# Optimizing a Trainium2 kernel written in Bass

```python
import jax, jax.numpy as jnp
from jax import lax
import numpy as np

D_MODEL = 1024
BATCH = 1
SEQ = 2048
DEPTH = 1

CHUNK = 64
NORM_EPS = 1e-6
L2_EPS = 1e-6
CONV_WIDTH = D_MODEL // 2
CONV_K = 3
HGRN_HEADS = 4
HGRN_DK = 128
HGRN_DV = 128
HGRN_WIDTH = HGRN_HEADS * HGRN_DK
GDN_QK_HEADS = 4
GDN_V_HEADS = 8
GDN_DK = 128
GDN_DV = 128
GDN_CONV_K = 4
GDN_QK_WIDTH = GDN_QK_HEADS * GDN_DK
GDN_V_WIDTH = GDN_V_HEADS * GDN_DV
N_BRANCHES = 3
IN_SPLITS = (CONV_WIDTH, CONV_WIDTH, CONV_WIDTH, CONV_WIDTH,
             HGRN_WIDTH, HGRN_WIDTH, HGRN_HEADS * HGRN_DV, HGRN_HEADS * HGRN_DV,
             GDN_QK_WIDTH, GDN_QK_WIDTH, GDN_V_WIDTH, GDN_V_HEADS, GDN_V_HEADS, GDN_V_WIDTH,
             N_BRANCHES * D_MODEL)
IN_COLS = sum(IN_SPLITS)
MIN_F = 1e-30

kernel_name = "hybrid_conv_hgrn2_gdn_gated_merge"

def rmsnorm(x, w):
    xf = x.astype(jnp.float32)
    y = xf * lax.rsqrt(jnp.mean(xf * xf, axis=-1, keepdims=True) + NORM_EPS)
    return (y * w.astype(jnp.float32)).astype(x.dtype)

def head_rmsnorm(o, w):
    return o * lax.rsqrt(jnp.mean(o * o, axis=-1, keepdims=True) + NORM_EPS) * w.astype(jnp.float32)

def l2norm(x):
    return x * lax.rsqrt(jnp.sum(x * x, axis=-1, keepdims=True) + L2_EPS)

def masked_exp(diff, mask):
    return jnp.where(mask, jnp.exp(jnp.where(mask, diff, 0.0)), 0.0)

def causal_dwconv(x, w):
    k = w.shape[0]
    return lax.conv_general_dilated(
        x, w[:, None, :].astype(x.dtype), window_strides=(1,), padding=((k - 1, 0),),
        dimension_numbers=('NWC', 'WIO', 'NWC'), feature_group_count=x.shape[-1])

def to_chunks(x, heads):
    b, s, hd = x.shape
    return x.reshape(b, s // CHUNK, CHUNK, heads, hd // heads).transpose(0, 3, 1, 2, 4)

def scalar_chunks(x):
    b, s, h = x.shape
    return x.reshape(b, s // CHUNK, CHUNK, h).transpose(0, 3, 1, 2)

def from_chunks(o):
    b, h, n, l, d = o.shape
    return o.transpose(0, 2, 3, 1, 4).reshape(b, n * l, h, d)

def hgrn2_chunked(q, k, v, log_f):
    g = jnp.cumsum(log_f, axis=-2)
    g_last = g[..., -1:, :]
    q_inter = q * jnp.exp(g)
    k_state = k * jnp.exp(g_last - g)
    causal = jnp.tril(jnp.ones((CHUNK, CHUNK), dtype=bool))[:, :, None]
    mv = lambda a: jnp.moveaxis(a, 2, 0)

    def step(state, inp):
        qc, kc, vc, gc, qi, ks, gl = inp
        diff = gc[..., :, None, :] - gc[..., None, :, :]
        decay = masked_exp(diff, causal)
        scores = jnp.einsum('bhtk,bhtsk,bhsk->bhts', qc, decay, kc)
        o = jnp.einsum('bhts,bhsv->bhtv', scores, vc) + jnp.einsum('bhtk,bhkv->bhtv', qi, state)
        state = jnp.exp(gl)[..., 0, :, None] * state + jnp.einsum('bhsk,bhsv->bhkv', ks, vc)
        return state, o

    b, h = q.shape[0], q.shape[1]
    s0 = jnp.zeros((b, h, q.shape[-1], v.shape[-1]), jnp.float32)
    _, o = lax.scan(step, s0, (mv(q), mv(k), mv(v), mv(g), mv(q_inter), mv(k_state), mv(g_last)))
    return jnp.moveaxis(o, 0, 2)

def gated_delta_chunked(q, k, v, log_a, beta):
    g = jnp.cumsum(log_a, axis=-1)
    g_last = g[..., -1]
    diff = g[..., :, None] - g[..., None, :]
    strict = jnp.tril(jnp.ones((CHUNK, CHUNK), dtype=bool), -1)
    causal = jnp.tril(jnp.ones((CHUNK, CHUNK), dtype=bool))
    decay_strict = masked_exp(diff, strict)
    decay_causal = masked_exp(diff, causal)
    kb = k * beta[..., None]
    m = jnp.einsum('bhntk,bhnsk->bhnts', k, kb) * decay_strict
    eye = jnp.eye(CHUNK, dtype=jnp.float32)
    rhs = jnp.concatenate([v, k * jnp.exp(g)[..., None]], axis=-1)
    sol = lax.linalg.triangular_solve(eye + m, rhs, left_side=True, lower=True, unit_diagonal=True)
    u, w = sol[..., :v.shape[-1]], sol[..., v.shape[-1]:]
    a_qk = jnp.einsum('bhntk,bhnsk->bhnts', q, kb) * decay_causal
    q_inter = q * jnp.exp(g)[..., None]
    k_state = kb * jnp.exp(g_last[..., None] - g)[..., None]
    mv = lambda a: jnp.moveaxis(a, 2, 0)

    def step(state, inp):
        uc, wc, aqk, qi, ks, gl = inp
        e = uc - jnp.einsum('bhlk,bhkv->bhlv', wc, state)
        o = jnp.einsum('bhlk,bhkv->bhlv', qi, state) + jnp.einsum('bhts,bhsv->bhtv', aqk, e)
        state = jnp.exp(gl)[..., None, None] * state + jnp.einsum('bhlk,bhlv->bhkv', ks, e)
        return state, o

    b, h = q.shape[0], q.shape[1]
    s0 = jnp.zeros((b, h, q.shape[-1], v.shape[-1]), jnp.float32)
    _, o = lax.scan(step, s0, (mv(u), mv(w), mv(a_qk), mv(q_inter), mv(k_state), mv(g_last)))
    return jnp.moveaxis(o, 0, 2)

def setup_inputs(seed: int = 0) -> dict:
    key = jax.random.key(seed)
    ks = jax.random.split(key, 16)
    f32 = jnp.float32
    nrm = lambda k, shape, scale: jax.random.normal(k, shape, f32) * scale
    dt = jnp.exp(jax.random.uniform(ks[7], (DEPTH, GDN_V_HEADS), f32, np.log(1e-3), np.log(1e-1)))
    return {
        "x": nrm(ks[0], (BATCH, SEQ, D_MODEL), 1.0),
        "norm_w": 1.0 + nrm(ks[1], (DEPTH, D_MODEL), 0.02),
        "w_in": nrm(ks[2], (DEPTH, D_MODEL, IN_COLS), D_MODEL ** -0.5),
        "b_gate": nrm(ks[3], (DEPTH, N_BRANCHES * D_MODEL), 0.1),
        "conv_a": nrm(ks[4], (DEPTH, CONV_K, CONV_WIDTH), CONV_K ** -0.5),
        "conv_c": nrm(ks[5], (DEPTH, GDN_CONV_K, 2 * GDN_QK_WIDTH + GDN_V_WIDTH), GDN_CONV_K ** -0.5),
        "a_log": jnp.log(jax.random.uniform(ks[6], (DEPTH, GDN_V_HEADS), f32, 1.0, 16.0)),
        "dt_bias": dt + jnp.log(-jnp.expm1(-dt)),
        "lower_bounds": nrm(ks[8], (DEPTH, HGRN_WIDTH), 0.5),
        "hgrn_norm_w": 1.0 + nrm(ks[9], (DEPTH, HGRN_DV), 0.02),
        "gdn_norm_w": 1.0 + nrm(ks[10], (DEPTH, GDN_DV), 0.02),
        "w_out_a": nrm(ks[11], (DEPTH, CONV_WIDTH, D_MODEL), CONV_WIDTH ** -0.5),
        "w_out_b": nrm(ks[12], (DEPTH, HGRN_HEADS * HGRN_DV, D_MODEL), (HGRN_HEADS * HGRN_DV) ** -0.5),
        "w_out_c": nrm(ks[13], (DEPTH, GDN_V_WIDTH, D_MODEL), GDN_V_WIDTH ** -0.5),
        "w_o": nrm(ks[14], (DEPTH, D_MODEL, D_MODEL), D_MODEL ** -0.5),
        "final_norm_w": 1.0 + nrm(ks[15], (D_MODEL,), 0.02),
    }

def reference(x, norm_w, w_in, b_gate, conv_a, conv_c, a_log, dt_bias, lower_bounds,
              hgrn_norm_w, gdn_norm_w, w_out_a, w_out_b, w_out_c, w_o, final_norm_w):
    f32 = jnp.float32
    bsz, seq = x.shape[0], x.shape[1]
    split_idx = tuple(int(s) for s in np.cumsum(IN_SPLITS)[:-1])
    p = jax.nn.softmax(lower_bounds.astype(f32), axis=0)
    lbs = jnp.cumsum(p, axis=0) - p[0]

    for l in range(DEPTH):
        h = rmsnorm(x, norm_w[l])
        proj = jnp.einsum('bsd,dc->bsc', h, w_in[l])
        (a_b, a_c, a_x, a_z, b_q, b_f, b_i, b_z,
         c_q, c_k, c_v, c_beta, c_a, c_z, g_all) = jnp.split(proj, split_idx, axis=-1)
        gates = jax.nn.sigmoid(g_all + b_gate[l]).reshape(bsz, seq, N_BRANCHES, D_MODEL)

        y_a = a_b * causal_dwconv(a_c * a_x, conv_a[l]) * jax.nn.silu(a_z)
        y_a = jnp.einsum('bsc,cd->bsd', y_a, w_out_a[l])

        lb = lbs[l].reshape(1, HGRN_HEADS, 1, 1, HGRN_DK)
        qb = to_chunks(jax.nn.silu(b_q.astype(f32)) * HGRN_DK ** -0.5, HGRN_HEADS)
        fz = to_chunks(b_f.astype(f32), HGRN_HEADS)
        f_gate = lb + (1.0 - lb) * jax.nn.sigmoid(fz)
        log_f = jnp.log(jnp.maximum(f_gate, MIN_F))
        kb = 1.0 - f_gate
        vb = to_chunks(b_i.astype(f32), HGRN_HEADS)
        o_b = from_chunks(hgrn2_chunked(qb, kb, vb, log_f))
        y_b = head_rmsnorm(o_b, hgrn_norm_w[l]).reshape(bsz, seq, -1) * jax.nn.silu(b_z.astype(f32))
        y_b = jnp.einsum('bsc,cd->bsd', y_b.astype(x.dtype), w_out_b[l])

        qkv = jax.nn.silu(causal_dwconv(jnp.concatenate([c_q, c_k, c_v], axis=-1), conv_c[l])).astype(f32)
        qc, kc, vc = jnp.split(qkv, (GDN_QK_WIDTH, 2 * GDN_QK_WIDTH), axis=-1)
        rep = GDN_V_HEADS // GDN_QK_HEADS
        qc = jnp.repeat(l2norm(qc.reshape(bsz, seq, GDN_QK_HEADS, GDN_DK)), rep, axis=2) * GDN_DK ** -0.5
        kc = jnp.repeat(l2norm(kc.reshape(bsz, seq, GDN_QK_HEADS, GDN_DK)), rep, axis=2)
        beta = jax.nn.sigmoid(c_beta.astype(f32))
        log_a = -jnp.exp(a_log[l].astype(f32)) * jax.nn.softplus(c_a.astype(f32) + dt_bias[l].astype(f32))
        o_c = gated_delta_chunked(
            to_chunks(qc.reshape(bsz, seq, -1), GDN_V_HEADS), to_chunks(kc.reshape(bsz, seq, -1), GDN_V_HEADS),
            to_chunks(vc, GDN_V_HEADS), scalar_chunks(log_a), scalar_chunks(beta))
        y_c = head_rmsnorm(from_chunks(o_c), gdn_norm_w[l]).reshape(bsz, seq, -1) * jax.nn.silu(c_z.astype(f32))
        y_c = jnp.einsum('bsc,cd->bsd', y_c.astype(x.dtype), w_out_c[l])

        merged = gates[:, :, 0] * y_a + gates[:, :, 1] * y_b + gates[:, :, 2] * y_c
        x = x + jnp.einsum('bsd,de->bse', merged, w_o[l])

    return rmsnorm(x, final_norm_w)


_drawn_inputs = setup_inputs


def setup_inputs(seed=0):
    import zlib

    import numpy as np

    out = dict(_drawn_inputs(seed))
    spreads = {}
    factors = {'norm_w': 3.089,
     'b_gate': 3.016,
     'hgrn_norm_w': 8.0,
     'gdn_norm_w': 8.0,
     'final_norm_w': 2.861}
    for name, (base, spread) in spreads.items():
        noise = np.random.default_rng([zlib.crc32(name.encode()), seed]).standard_normal(out[name].shape)
        drawn = base * np.exp(spread * noise) if base else spread * noise
        out[name] = __import__('jax').numpy.asarray(drawn.astype(out[name].dtype))
    for name, factor in factors.items():
        out[name] = (out[name] * factor).astype(out[name].dtype)
    return out
```

```python
from contextlib import ExitStack

import concourse.bass as bass
from concourse import mybir

F32 = mybir.dt.float32
F32R = mybir.dt.float32r
I32 = mybir.dt.int32
ALU = mybir.AluOpType
ACT = mybir.ActivationFunctionType

P = 128
BLK = 512
EPS = 1e-6
MIN_F = 1e-30
F_SPLIT = 2.0 ** -60
NEG_HALF = -0.5
TABLES = "natural_log_exp_and_others"
SILU_TABLES = "silu_and_others"
SIGMOID_TABLES = "sigmoid_and_others"


class Dims:

    def __init__(self, x, w_in, w_out_a, w_out_b, w_out_c):
        self.seq, self.d = x.shape[1], x.shape[2]
        self.cols = w_in.shape[2]
        self.kt = self.d // P
        self.wa = w_out_a.shape[1] // P
        self.hh = w_out_b.shape[1] // P
        self.vh = w_out_c.shape[1] // P
        self.qh = self.vh // 2
        self.win = self.seq // P
        self.blk = self.seq // BLK
        widths = [self.wa] * 4 + [self.hh] * 4 + [self.qh, self.qh, self.vh]
        at = [0]
        for n in widths:
            at.append(at[-1] + n * P)
        (self.a_b, self.a_c, self.a_x, self.a_z, self.b_q, self.b_f, self.b_i, self.b_z,
         self.c_q, self.c_k, self.c_v, self.c_beta) = at
        self.c_z = self.c_beta + 2 * self.vh
        self.gates = self.c_z + self.vh * P
        assert self.gates + 3 * self.d == self.cols


class Ahead:

    def __init__(self, sem, per, turns=1):
        self.sem, self.per, self.turns = sem, per, turns

    def credit(self, engine):
        engine.sem_inc(self.sem, self.per * self.turns)

    def at(self, turn, k):
        return turn * self.per + (self.per * self.turns + k)


def wait_apart(engine, sem, value, passed):
    engine.wait_ge(sem, value)
    engine.sem_inc(passed, 1)


def free_ap(ap, offset, dims):
    return bass.AP(ap.tensor, ap.offset + offset, [list(ap.ap[0])] + [list(x) for x in dims])


def across(ap, n):
    return free_ap(ap, 0, [[0, n], [1, ap.shape[-1]]])


def spread(ap, n):
    return free_ap(ap, 0, [[ap.ap[-1][0], ap.shape[-1]], [0, n]])


def vector_rows(dm):
    rows, at = {}, 0
    for name, n in (("norm_w", dm.kt), ("b_gate", 3 * dm.kt), ("conv_a", 3 * dm.wa),
                    ("conv_c", 4 * (2 * dm.qh + dm.vh)), ("lower", dm.hh), ("hgrn_w", 1), ("gdn_w", 1)):
        rows[name] = at
        at += n
    rows["end"] = at
    assert at <= P
    return rows


def constants(nc, dm, io, keep):
    rows = vector_rows(dm)
    n = rows["end"]
    with ExitStack() as c:
        vec = c.enter_context(nc.sbuf_tensor("vec", [P, P], F32))
        low = c.enter_context(nc.sbuf_tensor("low", [P, 4, dm.hh], F32))
        ps = c.enter_context(nc.psum_tensor("ps_vec", [P, P], F32))
        S = {k: c.enter_context(nc.semaphore("c_" + k)) for k in "loaded made turned copied low_exp low gave".split()}
        ident, ones, cols, eps = keep["ident"], keep["ones"], keep["cols"], keep["eps"]
        sources = [("norm_w", io["norm_w"].rearrange("l (r c) -> (l r) c", c=P)),
                   ("b_gate", io["b_gate"].rearrange("l (r c) -> (l r) c", c=P)),
                   ("conv_a", io["conv_a"].rearrange("l i (r c) -> (l i r) c", c=P)),
                   ("conv_c", io["conv_c"].rearrange("l i (r c) -> (l i r) c", c=P)),
                   ("lower", io["lower_bounds"].rearrange("l (r c) -> (l r) c", c=P)),
                   ("hgrn_w", io["hgrn_norm_w"]), ("gdn_w", io["gdn_norm_w"])]
        with nc.Block() as block:
            @block.sync
            def _(sp):
                for name, src in sources:
                    sp.dma_start(vec[rows[name]:rows[name] + src.shape[0], :], src).then_inc(S["loaded"], 16)
                for name, dst in (("a_log", keep["a_log"]), ("dt_bias", keep["dt_bias"])):
                    src = io[name]
                    sp.dma_start(dst[:], bass.AP(src.tensor, 0, [[0, P], [1, dm.vh]])).then_inc(S["loaded"], 16)
                sp.wait_ge(S["loaded"], 16 * (len(sources) + 2))

            @block.gpsimd
            def _(pool):
                pool.memset(ident[:], 0.0).then_inc(S["made"], 1)
                pool.memset(ones[:], 1.0).then_inc(S["made"], 1)
                pool.memset(eps[:], EPS).then_inc(S["made"], 1)
                pool.wait_ge(S["made"], 3)
                pool.affine_select(out=ident[:], in_=ident[:], compare_op=ALU.not_equal, fill=1.0, base=0,
                                   pattern=[[-1, P]], channel_multiplier=1).then_inc(S["made"], 1)

            @block.tensor
            def _(pe):
                pe.wait_ge(S["made"], 4)
                pe.wait_ge(S["loaded"], 16 * (len(sources) + 2))
                nc.tensor.transpose(ps[:, 0:n], vec[0:n, :], ident[0:n, 0:n]).then_inc(S["turned"], 1)

            @block.scalar
            def _(act):
                nc.scalar.preload_act_table_set(TABLES)
                act.wait_ge(S["low"], 1)
                nc.scalar.activation(low[:, 1, :], low[:, 0, :], ACT.Exp).then_inc(S["low_exp"], 1)

            @block.vector
            def _(dve):
                dve.wait_ge(S["turned"], 1)
                nc.vector.tensor_copy(cols[:, 0:n], ps[:, 0:n]).then_inc(S["copied"], 1)
                dve.wait_ge(S["copied"], 1)
                lw = cols[:, rows["lower"]:rows["lower"] + dm.hh]
                nc.vector.tensor_tensor(low[:, 0, :], lw, lw, ALU.subtract).then_inc(S["low"], 1)
                dve.wait_ge(S["low_exp"], 1)
                nc.vector.reciprocal(low[:, 2, :], low[:, 1, :]).then_inc(S["low"], 1)
                dve.wait_ge(S["low"], 2)
                nc.vector.tensor_tensor(low[:, 3, :], low[:, 1, :], low[:, 2, :], ALU.mult).then_inc(S["low"], 1)
                dve.wait_ge(S["low"], 3)
                nc.vector.tensor_tensor(keep["lb"][:], low[:, 3, :], low[:, 3, :], ALU.subtract).then_inc(S["low"], 1)
                dve.wait_ge(S["low"], 4)
                nc.vector.tensor_scalar(keep["one_less_lb"][:], keep["lb"][:], -1.0, 1.0, ALU.mult, ALU.add).then_inc(S["low"], 1)
                for k, name in enumerate(("hgrn_w", "gdn_w")):
                    nc.vector.tensor_scalar(keep["head_w"][:, k:k + 1], cols[:, rows[name]:rows[name] + 1], float(P) ** -0.5,
                                            None, ALU.mult).then_inc(S["low"], 1)


def norm_and_transpose(nc, dm, io, keep, hh, hl, h_dram):
    rows = vector_rows(dm)
    K, V = dm.kt, dm.vh
    with ExitStack() as c:
        sb = lambda n, s, d=F32: c.enter_context(nc.sbuf_tensor(n, s, d))
        xin, xn = sb("xin", [P, 2, dm.d]), sb("xn", [P, 2, dm.d])
        ht = sb("ht", [P, 2, K, P])
        wsm = sb("wsm", [P, K, 2 * V])
        stat = sb("stat", [P, 2, 3])
        z = sb("z", [P, 6, dm.win * V])
        ps = [c.enter_context(nc.psum_tensor(f"ps_h{i}", [P, BLK], F32)) for i in range(6)]
        sem = lambda n: c.enter_context(nc.semaphore("n_" + n))
        x_in = [Ahead(sem(f"x_in{u}"), 16) for u in range(2)]
        h_out = [Ahead(sem(f"h_out{u}"), 16) for u in range(2)]
        squared, rstd, scaled, turned = Ahead(sem("squared"), 1), Ahead(sem("rstd"), 2), Ahead(sem("scaled"), 1), Ahead(sem("turned"), 1)
        weighted, high, low, small, kept = Ahead(sem("weighted"), 2), Ahead(sem("high"), 1), Ahead(sem("low"), 1), Ahead(sem("small"), 1), Ahead(sem("kept"), 1)
        w_in, passed = sem("w_in"), sem("passed")
        tail_v, tail_a = sem("tail_v"), sem("tail_a")
        turns = dm.win // 2
        nw = keep["cols"][:, rows["norm_w"]:rows["norm_w"] + K]
        hd = h_dram.rearrange("k p n -> p k n")
        with nc.Block() as block:
            @block.sync
            def _(sp):
                sp.dma_start(wsm[:], io["w_in"][0, :, dm.c_beta:dm.c_beta + 2 * V].rearrange("(k p) c -> p k c", p=P)).then_inc(w_in, 16)
                for u in range(2):
                    h_out[u].credit(sp)
                with sp.Fori(0, turns) as i:
                    for u in range(2):
                        row = (i * 2 + u) * P
                        wait_apart(sp, scaled.sem, i * 2 + (u + 1), passed)
                        sp.dma_start(xin[:, u, :], io["x"][0, bass.ds(row, P), :]).then_inc(x_in[u].sem, 16)
                    for u in range(2):
                        w = i * 2 + u
                        row = w * P
                        wait_apart(sp, weighted.sem, weighted.at(w, 2), passed)
                        sp.dma_start(hd[:, :, bass.ds(row, P)], ht[:, u, :, :]).then_inc(h_out[u].sem, 16)
                for u in range(2):
                    sp.wait_ge(h_out[u].sem, 16 * turns + 16)
                sp.wait_ge(w_in, 16)

            @block.scalar
            def _(act):
                nc.scalar.preload_act_table_set(TABLES)
                for t in (squared, rstd, high):
                    t.credit(act)
                with act.Fori(0, turns) as i:
                    for u in range(2):
                        w = i * 2 + u
                        act.wait_ge(x_in[u].sem, i * 16 + 16)
                        act.wait_ge(scaled.sem, w + 1)
                        act.wait_ge(turned.sem, turned.at(w, 0))
                        nc.scalar.activation(xn[:, u, :], xin[:, u, :], ACT.Square, accum_out=stat[:, u, 0:1]).then_inc(squared.sem, 1)
                        act.wait_ge(squared.sem, squared.at(w, 1))
                        nc.scalar.activation(stat[:, u, 1:2], stat[:, u, 0:1], ACT.Ln, scale=1.0 / dm.d, bias=keep["eps"][:, 0:1]).then_inc(rstd.sem, 1)
                        act.wait_ge(rstd.sem, rstd.at(w, 1))
                        nc.scalar.activation(stat[:, u, 2:3], stat[:, u, 1:2], ACT.Exp, scale=NEG_HALF).then_inc(rstd.sem, 1)
                    for u in range(2):
                        w = i * 2 + u
                        act.wait_ge(weighted.sem, weighted.at(w, 2))
                        nc.scalar.activation(hh[:, :, bass.ds(w * P, P)], ht[:, u, :, :], ACT.Copy).then_inc(high.sem, 1)
                act.wait_ge(tail_v, 3)
                nc.scalar.activation(z[:, 1, :], z[:, 0, :], ACT.Exp, scale=-1.0).then_inc(tail_a, 1)
                nc.scalar.activation(z[:, 4, :], z[:, 3, :], ACT.Exp).then_inc(tail_a, 1)
                nc.scalar.activation(keep["a_log"][:], keep["a_log"][:], ACT.Exp).then_inc(tail_a, 1)
                act.wait_ge(tail_a, 2)
                nc.scalar.activation(z[:, 5, :], z[:, 4, :], ACT.Ln, bias=1.0).then_inc(tail_a, 1)

            @block.gpsimd
            def _(pool):
                low.credit(pool)
                with pool.Fori(0, turns) as i:
                    for u in range(2):
                        w = i * 2 + u
                        pool.wait_ge(high.sem, high.at(w, 1))
                        cut = bass.ds(w * P, P)
                        nc.gpsimd.tensor_tensor(hl[:, :, cut], ht[:, u, :, :], hh[:, :, cut].bitcast(F32), ALU.subtract).then_inc(low.sem, 1)

            @block.tensor
            def _(pe):
                for t in (turned, small):
                    t.credit(pe)
                pe.wait_ge(w_in, 16)
                with pe.Fori(0, turns) as i:
                    for u in range(2):
                        w = i * 2 + u
                        pe.wait_ge(scaled.sem, w + 3)
                        pe.wait_ge(weighted.sem, weighted.at(w, 0))
                        for k in range(K):
                            t = nc.tensor.transpose(ps[2 * u + k // 4][:, (k % 4) * P:(k % 4 + 1) * P], xn[:, u, k * P:(k + 1) * P], keep["ident"][:])
                        t.then_inc(turned.sem, 1)
                    for u in range(2):
                        w = i * 2 + u
                        pe.wait_ge(weighted.sem, weighted.at(w, 2))
                        pe.wait_ge(kept.sem, kept.at(w, 0))
                        for k in range(K):
                            t = nc.tensor.matmul(ps[4 + u][:, 0:2 * V], ht[:, u, k, :], wsm[:, k, :], start=(k == 0), stop=(k == K - 1))
                        t.then_inc(small.sem, 1)

            @block.vector
            def _(dve):
                scaled_credit = 2
                dve.sem_inc(scaled.sem, scaled_credit)
                for t in (weighted, kept):
                    t.credit(dve)
                with dve.Fori(0, turns) as i:
                    for u in range(2):
                        w = i * 2 + u
                        dve.wait_ge(rstd.sem, rstd.at(w, 2))
                        nc.vector.tensor_scalar(xn[:, u, :], xin[:, u, :], stat[:, u, 2:3], None, ALU.mult).then_inc(scaled.sem, 1)
                    for u in range(2):
                        w = i * 2 + u
                        dve.wait_ge(turned.sem, turned.at(w, 1))
                        dve.wait_ge(h_out[u].sem, i * 16 + 16)
                        dve.wait_ge(low.sem, low.at(w, 0))
                        dve.wait_ge(small.sem, small.at(w, 0))
                        for b in range(2):
                            nc.vector.tensor_tensor(ht[:, u, 4 * b:4 * b + 4, :], ps[2 * u + b][:].rearrange("p (k n) -> p k n", n=P),
                                                    spread(nw[:, 4 * b:4 * b + 4], P), ALU.mult).then_inc(weighted.sem, 1)
                    for u in range(2):
                        w = i * 2 + u
                        dve.wait_ge(small.sem, small.at(w, 1))
                        nc.vector.tensor_copy(keep["ab"][:, bass.ds(w * 2 * V, 2 * V)], ps[4 + u][:, 0:2 * V]).then_inc(kept.sem, 1)
                dve.wait_ge(kept.sem, kept.at(dm.win, 0))
                ab = keep["ab"][:, 0:dm.win * 2 * V].rearrange("p (w c) -> p w c", c=2 * V)
                zz = lambda k: z[:, k, :].rearrange("p (w c) -> p w c", c=V)
                over = lambda t: free_ap(t[:], 0, [[0, dm.win], [1, V]])
                nc.vector.tensor_copy(zz(0), ab[:, :, 0:V]).then_inc(tail_v, 1)
                nc.vector.tensor_tensor(zz(2), ab[:, :, V:2 * V], over(keep["dt_bias"]), ALU.add).then_inc(tail_v, 1)
                dve.wait_ge(tail_v, 2)
                nc.vector.scalar_tensor_tensor(z[:, 3, :], z[:, 2, :], -1.0, z[:, 2, :], ALU.mult, ALU.min).then_inc(tail_v, 1)
                dve.wait_ge(tail_a, 4)
                dve.wait_ge(tail_v, 3)
                nc.vector.scalar_tensor_tensor(z[:, 2, :], z[:, 2, :], 0.0, z[:, 5, :], ALU.max, ALU.add).then_inc(tail_v, 1)
                nc.vector.tensor_scalar(z[:, 1, :], z[:, 1, :], 1.0, None, ALU.add).then_inc(tail_v, 1)
                nc.vector.tensor_scalar(keep["a_log"][:], keep["a_log"][:], -1.0, None, ALU.mult).then_inc(tail_v, 1)
                dve.wait_ge(tail_v, 6)
                nc.vector.memset(keep["ab"][:, dm.win * 2 * V:], 0.0).then_inc(tail_v, 1)
                nc.vector.reciprocal(z[:, 0, :], z[:, 1, :]).then_inc(tail_v, 1)
                nc.vector.tensor_tensor(ab[:, :, 0:V], zz(2), over(keep["a_log"]), ALU.mult).then_inc(tail_v, 1)
                dve.wait_ge(tail_v, 9)
                nc.vector.tensor_copy(ab[:, :, V:2 * V], zz(0)).then_inc(tail_v, 1)


def branch_tiles(dm):
    at, n = {}, 0
    for name, k in (("hk", dm.hh), ("hq", dm.hh), ("h_neg_g", dm.hh), ("hg", dm.hh), ("hv", dm.hh), ("hz", dm.hh),
                    ("q", dm.qh), ("k", dm.qh), ("v", dm.vh), ("z", dm.vh)):
        at[name] = n
        n += k
    at["end"] = n
    return at


def pass_on(engine, sem, value, *others):
    engine.wait_ge(sem, value)
    for other in others:
        engine.sem_inc(other, 1)


def project(nc, dm, io, keep, hh, hl, s_dram, y_dram):
    rows, tiles, K, T = vector_rows(dm), branch_tiles(dm), dm.kt, dm.blk
    groups = dm.wa
    assert dm.wa == dm.hh == dm.qh and T == 4
    units = [("copy_c", dm.a_c, 1, None), ("x", dm.a_x, 1, None), ("gate_a", dm.a_z, 1, None), ("b", dm.a_b, 1, None),
             ("silu", dm.b_q, 1, tiles["hq"]), ("forget", dm.b_f, 1, None), ("plain", dm.b_i, 1, tiles["hv"]),
             ("silu", dm.b_z, 1, tiles["hz"]), ("conv", dm.c_q, 1, tiles["q"]), ("conv", dm.c_k, 1, tiles["k"]),
             ("conv", dm.c_v, 2, tiles["v"]), ("conv", dm.c_v + P, 2, tiles["v"] + 1),
             ("silu", dm.c_z, 2, tiles["z"]), ("silu", dm.c_z + P, 2, tiles["z"] + 1)]
    U = len(units)
    conv_tile = {8: (0, 1), 9: (dm.qh, 1), 10: (2 * dm.qh, 2), 11: (2 * dm.qh + 1, 2)}
    results = []
    for m, (kind, *_) in enumerate(units):
        for t in range(T):
            results += [(m, t, part) for part in {"copy_c": [], "x": [], "gate_a": [], "forget": ["k", "g", "neg_g"]}.get(kind, ["y"])]
    RING = 4
    assert len(results) % RING == 0
    uses = len(results) // RING
    from_dve = [r for r in results if units[r[0]][0] in ("b", "forget")]

    def per_unit(kinds):
        return [m for m, u in enumerate(units) if u[0] in kinds]

    class Steps:

        def __init__(self, sem, kinds):
            self.sem, self.of = sem, per_unit(kinds)

        def at(self, group, m, t):
            return group * (T * len(self.of)) + (T * self.of.index(m) + t + 1)

    with ExitStack() as c:
        sb = lambda n, s, d=F32: c.enter_context(nc.sbuf_tensor(n, s, d))
        stage = sb("w_stage", [P, 2, K, P])
        wh, wl = sb("w_high", [P, 2, K, P], F32R), sb("w_low", [P, 2, K, P], F32R)
        hist = sb("hist", [P, 2, 3 + dm.seq])
        cb = sb("cb", [P, T, BLK])
        act_z = sb("act_z", [P, 2, BLK])
        ex = sb("ex", [P, 2, BLK])
        tap = sb("tap", [P, 2, BLK])
        fg = sb("fg", [P, 2, BLK])
        ring = sb("ring", [P, RING, BLK])
        fresh = sb("fresh", [P, BLK])
        ps = [c.enter_context(nc.psum_tensor(f"ps_p{i}", [P, BLK], F32)) for i in range(T)]
        sem = lambda n: c.enter_context(nc.semaphore("p_" + n))
        w_in = [sem(f"w_in{s}") for s in range(2)]
        w_high = sem("w_high")
        w_ready, acc = Ahead(sem("w_ready"), 1, 2), Ahead(sem("acc"), T, 2)
        bank_free = [Ahead(sem(f"bank_free{t}"), 1, 1) for t in range(T)]
        copied = Steps(sem("copied"), ("copy_c", "plain", "conv"))
        silued = Steps(sem("silued"), ("gate_a", "silu", "conv"))
        gated = Steps(sem("gated"), ("gate_a",))
        exped = Steps(sem("exped"), ("forget",))
        tapped = Steps(sem("tapped"), ("conv",))
        ranged, logged = Steps(sem("ranged"), ("forget",)), Steps(sem("logged"), ("forget",))
        ready = sem("ready")
        out_done = [sem(f"out_done{r}") for r in range(RING)]
        zeroed, step, passed, passed_p = sem("zeroed"), sem("step"), sem("passed"), sem("passed_p")

        def slot(m, t, part):
            return results.index((m, t, part)) % RING

        def free_value(g, m, t, part):
            return g * (16 * uses) + (16 * (results.index((m, t, part)) // RING) + 16)

        def ready_value(g, m, t, part):
            return g * len(from_dve) + (from_dve.index((m, t, part)) + 1)

        def unit_no(g, m):
            return g * U + m

        with nc.Block() as block:
            @block.sync
            def _(sp):
                with sp.Fori(0, groups) as g:
                    for m, (_, col, by, _) in enumerate(units):
                        wait_apart(sp, w_ready.sem, w_ready.at(unit_no(g, m), -1), passed)
                        sp.dma_start(stage[:, m % 2, :, :], io["w_in"][0, :, bass.ds(g * (by * P) + col, P)].rearrange("(k p) c -> p k c", p=P)
                                     ).then_inc(w_in[m % 2], 16)

            @block.gpsimd
            def _(pool):
                w_ready.credit(pool)
                pool.memset(hist[:, :, 0:3], 0.0).then_inc(zeroed, 1)
                pool.memset(fresh[:], 1.0).then_inc(zeroed, 1)
                pool.wait_ge(zeroed, 2)
                pool.memset(free_ap(fresh[:], 0, [[P, BLK // P], [1, 1]]), 0.0).then_inc(zeroed, 1)
                with pool.Fori(0, groups * U // 2) as i:
                    for s in range(2):
                        n = i * 2 + s
                        pool.wait_ge(acc.sem, acc.at(n, -T))
                        wait_apart(pool, w_in[s], i * 16 + 16, passed_p)
                        nc.gpsimd.tensor_scalar(wh[:, s, :, :], stage[:, s, :, :], 1.0, None, ALU.mult).then_inc(w_high, 1)
                        pool.wait_ge(w_high, n + 1)
                        nc.gpsimd.tensor_tensor(wl[:, s, :, :], stage[:, s, :, :], wh[:, s, :, :].bitcast(F32), ALU.subtract).then_inc(w_ready.sem, 1)

            @block.tensor
            def _(pe):
                acc.credit(pe)
                with pe.Fori(0, groups * U // 2) as i:
                    for s in range(2):
                        n = i * 2 + s
                        pe.wait_ge(w_ready.sem, w_ready.at(n, 1))
                        for t in range(T):
                            pe.wait_ge(bank_free[t].sem, bank_free[t].at(n, 0))
                            cut = slice(t * BLK, (t + 1) * BLK)
                            for k in range(K):
                                for a, (w, h) in enumerate(((wh, hh), (wl, hh), (wh, hl))):
                                    last = nc.tensor.matmul(ps[t][:], w[:, s, k, :], h[:, k, cut], start=(k == 0 and a == 0),
                                                            stop=(k == K - 1 and a == 2))
                            last.then_inc(acc.sem, 1)

            @block.scalar
            def _(act):
                nc.scalar.preload_act_table_set(TABLES)
                for r in range(RING):
                    act.sem_inc(out_done[r], 16)
                act.wait_ge(zeroed, 3)
                with act.Fori(0, groups) as g:
                    def store(m, t, part, tile, by, dram):
                        kind, r = units[m][0], slot(m, t, part)
                        if kind == "plain":
                            act.wait_ge(copied.sem, copied.at(g, m, t))
                        elif kind in ("silu", "conv"):
                            act.wait_ge(silued.sem, silued.at(g, m, t))
                        else:
                            act.wait_ge(ready, ready_value(g, m, t, part))
                        nc.scalar.dma_start(dram[bass.ds(g * by + tile, 1), :, t * BLK:(t + 1) * BLK].rearrange("o p n -> p (o n)"),
                                            ring[:, r, :]).then_inc(out_done[r], 16)

                    nc.scalar.preload_act_table_set(SILU_TABLES)
                    for m, (kind, _, by, tile) in enumerate(units):
                        n = unit_no(g, m)
                        if kind == "forget":
                            nc.scalar.preload_act_table_set(TABLES)
                        for t in range(T + 2):
                            bank, cut = t < T, slice(3 + t * BLK, 3 + (t + 1) * BLK)
                            if bank and kind not in ("x", "b"):
                                act.wait_ge(acc.sem, acc.at(n, t + 1))
                            if kind == "copy_c" and bank:
                                nc.scalar.activation(cb[:, t, :], ps[t][:], ACT.Copy).then_inc(copied.sem, 1)
                                pass_on(act, copied.sem, copied.at(g, m, t), bank_free[t].sem)
                            elif kind == "gate_a" and bank:
                                if t >= 2:
                                    act.wait_ge(gated.sem, gated.at(g, m, t - 2))
                                nc.scalar.activation(act_z[:, t % 2, :], ps[t][:], ACT.Silu).then_inc(silued.sem, 1)
                                pass_on(act, silued.sem, silued.at(g, m, t), bank_free[t].sem)
                            elif kind == "b" and bank:
                                store(m, t, "y", 0, 1, y_dram)
                            elif kind in ("silu", "plain"):
                                if bank:
                                    func, done = (ACT.Silu, silued) if kind == "silu" else (ACT.Copy, copied)
                                    act.wait_ge(out_done[slot(m, t, "y")], free_value(g, m, t, "y"))
                                    nc.scalar.activation(ring[:, slot(m, t, "y"), :], ps[t][:], func).then_inc(done.sem, 1)
                                    pass_on(act, done.sem, done.at(g, m, t), bank_free[t].sem)
                                if 1 <= t <= T:
                                    store(m, t - 1, "y", tile, by, s_dram)
                            elif kind == "forget":
                                if bank:
                                    nc.scalar.activation(ex[:, t % 2, :], ps[t][:], ACT.Exp, scale=-1.0).then_inc(exped.sem, 1)
                                    pass_on(act, exped.sem, exped.at(g, m, t), bank_free[t].sem)
                                    act.wait_ge(ranged.sem, ranged.at(g, m, t))
                                    nc.scalar.activation(fg[:, 0, :], fg[:, 0, :], ACT.Ln)
                                    nc.scalar.activation(fg[:, 1, :], fg[:, 1, :], ACT.Ln, scale=1.0 / F_SPLIT).then_inc(logged.sem, 1)
                                if 1 <= t <= T:
                                    for part, where in (("k", "hk"), ("g", "hg"), ("neg_g", "h_neg_g")):
                                        store(m, t - 1, part, tiles[where], 1, s_dram)
                            elif kind == "conv":
                                if bank:
                                    nc.scalar.activation(hist[:, m % 2, cut], ps[t][:], ACT.Copy).then_inc(copied.sem, 1)
                                    pass_on(act, copied.sem, copied.at(g, m, t), bank_free[t].sem)
                                if 1 <= t <= T:
                                    act.wait_ge(tapped.sem, tapped.at(g, m, t - 1))
                                    act.wait_ge(out_done[slot(m, t - 1, "y")], free_value(g, m, t - 1, "y"))
                                    nc.scalar.activation(ring[:, slot(m, t - 1, "y"), :], tap[:, (t - 1) % 2, :], ACT.Silu).then_inc(silued.sem, 1)
                                if t >= 2:
                                    store(m, t - 2, "y", tile, by, s_dram)
                        if kind == "forget":
                            nc.scalar.preload_act_table_set(SILU_TABLES)
                for r in range(RING):
                    act.wait_ge(out_done[r], 16 * uses * groups + 16)

            @block.vector
            def _(dve):
                for t in range(T):
                    bank_free[t].credit(dve)
                dve.wait_ge(zeroed, 3)
                links = 84
                with dve.Fori(0, groups) as g:
                    chain = [0]

                    def link(ins):
                        chain[0] += 1
                        ins.then_inc(step, 1)
                        dve.wait_ge(step, g * links + chain[0])

                    col = lambda name, i, at, by: keep["cols"][:, bass.ds(g * by + (rows[name] + i + at), 1)]
                    for m, (kind, _, by, tile) in enumerate(units):
                        n = unit_no(g, m)

                        def result(t, part="y"):
                            r = slot(m, t, part)
                            dve.wait_ge(out_done[r], free_value(g, m, t, part))
                            return ring[:, r, :]

                        def conv(out, h, t, taps, name, at, by):
                            per_tap = keep_tiles[name]
                            for i in range(taps):
                                src = hist[:, h, 3 + t * BLK - (taps - 1 - i):3 + (t + 1) * BLK - (taps - 1 - i)]
                                w = col(name, i * per_tap, at, by)
                                if i == 0:
                                    link(nc.vector.tensor_scalar(out, src, w, None, ALU.mult))
                                elif i < taps - 1:
                                    link(nc.vector.scalar_tensor_tensor(out, src, w, out, ALU.mult, ALU.add))
                                else:
                                    return nc.vector.scalar_tensor_tensor(out, src, w, out, ALU.mult, ALU.add)

                        keep_tiles = {"conv_a": dm.wa, "conv_c": 2 * dm.qh + dm.vh}
                        if kind == "x":
                            for t in range(T):
                                dve.wait_ge(copied.sem, copied.at(g, 0, t))
                                dve.wait_ge(acc.sem, acc.at(n, t + 1))
                                link(nc.vector.tensor_tensor(hist[:, 1, 3 + t * BLK:3 + (t + 1) * BLK], cb[:, t, :], ps[t][:], ALU.mult))
                                dve.sem_inc(bank_free[t].sem, 1)
                                link(conv(cb[:, t, :], 1, t, 3, "conv_a", 0, 1))
                        elif kind == "gate_a":
                            for t in range(T):
                                dve.wait_ge(silued.sem, silued.at(g, m, t))
                                nc.vector.tensor_tensor(cb[:, t, :], cb[:, t, :], act_z[:, t % 2, :], ALU.mult).then_inc(gated.sem, 1)
                        elif kind == "b":
                            for t in range(T):
                                if t == 0:
                                    dve.wait_ge(gated.sem, gated.at(g, m - 1, T - 1))
                                dve.wait_ge(acc.sem, acc.at(n, t + 1))
                                nc.vector.tensor_tensor(result(t), ps[t][:], cb[:, t, :], ALU.mult).then_inc(ready, 1)
                                pass_on(dve, ready, ready_value(g, m, t, "y"), bank_free[t].sem)
                        elif kind == "forget":
                            for t in range(T):
                                e = ex[:, t % 2, :]
                                dve.wait_ge(exped.sem, exped.at(g, m, t))
                                link(nc.vector.tensor_scalar(e, e, 1.0, None, ALU.add))
                                link(nc.vector.reciprocal(e, e))
                                link(nc.vector.tensor_scalar(e, e, keep["one_less_lb"][:, bass.ds(g, 1)], keep["lb"][:, bass.ds(g, 1)], ALU.mult, ALU.add))
                                nc.vector.tensor_scalar(result(t, "k"), e, -1.0, 1.0, ALU.mult, ALU.add).then_inc(ready, 1)
                                link(nc.vector.tensor_scalar(fg[:, 1, :], e, MIN_F, F_SPLIT, ALU.max, ALU.min))
                                nc.vector.tensor_scalar(fg[:, 0, :], e, F_SPLIT, None, ALU.max).then_inc(ranged.sem, 1)
                                dve.wait_ge(logged.sem, logged.at(g, m, t))
                                link(nc.vector.tensor_tensor(fg[:, 0, :], fg[:, 0, :], fg[:, 1, :], ALU.add))
                                out = result(t, "g")
                                nc.vector.tensor_tensor_scan(out, fresh[:], fg[:, 0, :], 0.0, ALU.mult, ALU.add).then_inc(ready, 1)
                                dve.wait_ge(ready, ready_value(g, m, t, "g"))
                                nc.vector.tensor_scalar(result(t, "neg_g"), out, -1.0, None, ALU.mult).then_inc(ready, 1)
                        elif kind == "conv":
                            at, by_c = conv_tile[m]
                            for t in range(T):
                                dve.wait_ge(copied.sem, copied.at(g, m, t))
                                if t >= 2:
                                    dve.wait_ge(silued.sem, silued.at(g, m, t - 2))
                                conv(tap[:, t % 2, :], m % 2, t, 4, "conv_c", at, by_c).then_inc(tapped.sem, 1)
                    assert chain[0] == links, chain[0]


def fill_masks(nc, keep, at):
    causal, later, pair, upper, lower = (at[k] for k in ("causal", "later", "pair", "upper", "lower"))
    with nc.semaphore("k_ones") as ones, nc.semaphore("k_cut") as cut, nc.Block() as block:
        @block.gpsimd
        def _(pool):
            pool.memset(causal[:], 1.0).then_inc(ones, 1)
            pool.memset(later[:], 1.0).then_inc(ones, 1)
            pool.memset(pair[:, 0, :], 1.0).then_inc(ones, 1)
            pool.memset(pair[:, 1, :], -1.0).then_inc(ones, 1)
            pool.memset(upper[:], 0.0).then_inc(ones, 1)
            pool.memset(lower[:], 0.0).then_inc(ones, 1)
            pool.wait_ge(ones, 6)
            levels = upper.shape[1]

            def half(mask, l, right):
                b = 1 << l
                return free_ap(mask[:, l, :], b if right else 0, [[2 * b, P // (2 * b)], [1, b]])

            for l in range(levels):
                pool.memset(half(upper, l, True), 1.0).then_inc(ones, 1)
                pool.memset(half(lower, l, False), 1.0).then_inc(ones, 1)
            pool.wait_ge(ones, 6 + 2 * levels)
            n = 0

            def select(ap, op, base, pattern, by):
                nonlocal n
                n += 1
                pool.affine_select(out=ap, in_=ap, compare_op=op, fill=0.0, base=base, pattern=pattern,
                                   channel_multiplier=by).then_inc(cut, 1)
                pool.wait_ge(cut, n)

            select(causal[:], ALU.is_ge, 0, [[1, P]], -1)
            select(later[:], ALU.is_gt, 0, [[-1, P]], 1)
            select(pair[:, 0, :], ALU.is_ge, 0, [[1, P]], -1)
            select(pair[:, 1, :], ALU.is_gt, 0, [[1, P]], -1)
            for l in range(levels):
                b = 1 << l
                blocks = P // (2 * b)
                for mask, right, first in ((upper, True, 0), (lower, False, b)):
                    ap = half(mask, l, right)
                    select(ap, ALU.is_ge, -first, [[-2 * b, blocks], [0, b]], 1)
                    select(ap, ALU.is_ge, first + b - 1, [[2 * b, blocks], [0, b]], -1)


def recur(nc, dm, keep, s_dram, y_dram):
    tiles, H, Q, V = branch_tiles(dm), dm.hh, dm.qh, dm.vh
    assert H == 4 and Q == 4 and V == 8
    NH, NC = 6 * H, 2 * Q + 2 * V
    KH, QH, NG, GG, VH, ZH = (tiles[k] for k in ("hk", "hq", "h_neg_g", "hg", "hv", "hz"))
    QC, VC, ZC = 0, 2 * Q, 2 * Q + V
    LEVELS = 7
    HOP = H * P
    last = P - 1
    hw = keep["head_w"]
    with ExitStack() as c:
        sb = lambda n, s, d=F32: c.enter_context(nc.sbuf_tensor(n, s, d))
        masks = {"causal": sb("causal", [P, P]), "later": sb("later", [P, P]), "pair": sb("pair", [P, 2, P]),
                 "upper": sb("upper", [P, LEVELS, P]), "lower": sb("lower", [P, LEVELS, P])}
        fill_masks(nc, keep, masks)
        hin, cin = sb("hin", [P, 2, NH, P]), sb("cin", [P, 2, NC, P])
        lbw = sb("lbw", [P, 2 * V])
        la_t = sb("la_t", [P, V, P])
        dec, eg = sb("dec", [P, V, P]), sb("eg", [P, V, P])
        ecol = sb("ecol", [P, 2 * V])
        neg_eg, bk = sb("neg_eg", [P, V]), sb("bk", [P, V])
        sq, rn, qkn = sb("sq", [P, 2, Q * P]), sb("rn", [P, 2, Q * P]), sb("qkn", [P, 2, Q * P])
        kqm = sb("kqm", [P, Q, 2 * P])
        an = sb("an", [P, V, 2, P])
        R, TT, W = sb("R", [P, V, P]), sb("T", [P, V, P]), sb("W", [P, V, P])
        vt, kt = sb("vt", [P, V, P]), sb("kt", [P, Q, P])
        qg, ks, r, e = sb("qg", [P, V, P]), sb("ks", [P, V, P]), sb("r", [P, V, P]), sb("e", [P, V, P])
        S, sqc, rnc, t1c = sb("S", [P, V, P]), sb("sqc", [P, V, P]), sb("rnc", [P, V, P]), sb("t1c", [P, V, P])
        yc, yh = sb("yc", [P, 2, V, P]), sb("yh", [P, 2, H, P])
        dx, hx, kql = sb("dx", [P, 2, HOP]), sb("hx", [P, 2, HOP]), sb("kql", [P, 2, HOP])
        egh, qe, ke, A = sb("egh", [P, H, P]), sb("qe", [P, HOP]), sb("ke", [P, H, P]), sb("A", [P, H, P])
        vht, kht, sqh, rnh, t1h, SH = (sb(n, [P, H, P]) for n in ("vht", "kht", "sqh", "rnh", "t1h", "SH"))
        bank = lambda n: c.enter_context(nc.psum_tensor("b_" + n, [P, 4, P], F32))
        G, HB, M = [bank(f"g{i}") for i in range(2)], [bank(f"h{i}") for i in range(2)], [bank(f"m{i}") for i in range(4)]

        sems = {}

        def count(engine, **per):
            for n, k in per.items():
                sems[n] = (Ahead(c.enter_context(nc.semaphore("r_" + n)), k), engine)

        count("pe", m_col=1, m_g=4, m_ssq=2, m_vt=2, m_kq=2, m_kt=1, m_t=2, m_w=12, m_z=12, m_r=10, m_hs=8, m_ks=2,
              m_hvt=1, m_hkt=1, m_ho=1, m_hds=1, m_e=2, m_o=2, m_ds=2, m_hn=1, m_n=2)
        count("act", e_col=1, e_g=4, rn_ready=4, e_h=1, vt_ready=2, kt_ready=1, t_ready=2, w_ready=12, r_ready=10,
              h_exp=8, h_turned=2, e_ready=2, sqh_ready=1, sqc_ready=2, rnh_ready=2, rnc_ready=4)
        count("pool", sq_ready=1, r_init=1, dx_ready=8, qe_ready=1, ke_ready=1, qg_ready=1, ks_ready=1)
        count("dve", lb=1, la_ready=1, qkn_ready=2, cols_ready=2, kqm_ready=2, an_ready=8, r_pair=2, h_kq=7, h_pred=8,
              t_pred=10, r_done=2, res=8, hs_done=4, t1h_ready=1, y_h=1, s_done=8, t1c_ready=2, y_c=2)
        h_in = [c.enter_context(nc.semaphore(f"r_h_in{u}")) for u in range(2)]
        c_in = [c.enter_context(nc.semaphore(f"r_c_in{u}")) for u in range(2)]
        yh_out = [c.enter_context(nc.semaphore(f"r_yh_out{u}")) for u in range(2)]
        yc_out = [c.enter_context(nc.semaphore(f"r_yc_out{u}")) for u in range(2)]
        s_zero, passed, passed_sp = (c.enter_context(nc.semaphore("r_" + n)) for n in ("s_zero", "passed", "passed_sp"))

        def wait(engine, w, name, k):
            engine.wait_ge(sems[name][0].sem, sems[name][0].at(w, k))

        def sem(name):
            return sems[name][0].sem

        def credits(engine, name):
            for t, of in sems.values():
                if of == name:
                    t.credit(engine)

        flat = lambda t: t[:].rearrange("p a b -> p (a b)")
        four = lambda t, g: t[:, 4 * g:4 * g + 4, :]

        def level_ap(tile, u, at, off, hop, inner):
            return free_ap(tile[:, u, at, :], off, [hop[0], hop[1], inner])

        turns = dm.win // 2
        ds = dm.win
        with nc.Block() as block:
            @block.sync
            def _(sp):
                for u in range(2):
                    sp.sem_inc(yh_out[u], 16)
                    sp.sem_inc(yc_out[u], 16)
                n_h = 6 * H

                def load(w, u):
                    cut = bass.ds(w * P, P)
                    sp.dma_start(hin[:, u, :, :], s_dram[0:n_h, :, cut].rearrange("t p n -> p t n")).then_inc(h_in[u], 16)
                    sp.dma_start(cin[:, u, :, :], s_dram[n_h:n_h + NC, :, cut].rearrange("t p n -> p t n")).then_inc(c_in[u], 16)

                def store(w, u):
                    cut = bass.ds(w * P, P)
                    wait_apart(sp, sem("y_h"), sems["y_h"][0].at(w, 1), passed_sp)
                    sp.dma_start(y_dram[dm.wa:dm.wa + H, :, cut].rearrange("t p n -> p t n"), yh[:, u, :, :]).then_inc(yh_out[u], 16)
                    wait_apart(sp, sem("y_c"), sems["y_c"][0].at(w, 2), passed_sp)
                    sp.dma_start(y_dram[dm.wa + H:dm.wa + H + V, :, cut].rearrange("t p n -> p t n"), yc[:, u, :, :]).then_inc(yc_out[u], 16)

                for u in range(2):
                    load(u, u)
                with sp.Fori(0, turns - 1) as i:
                    for u in range(2):
                        store(i * 2 + u, u)
                        load(i * 2 + (u + 2), u)
                for u in range(2):
                    store(dm.win - 2 + u, u)
                for u in range(2):
                    sp.wait_ge(yh_out[u], 16 * turns + 16)
                    sp.wait_ge(yc_out[u], 16 * turns + 16)

            @block.gpsimd
            def _(pool):
                credits(pool, "pool")
                tt = nc.gpsimd.tensor_tensor
                with pool.Fori(0, turns) as i:
                    for u in range(2):
                        w = i * 2 + u
                        pool.wait_ge(h_in[u], i * 16 + 16)
                        pool.wait_ge(c_in[u], i * 16 + 16)
                        wait(pool, w, "m_ssq", 0)
                        qk = cin[:, u, QC:QC + 2 * Q, :]
                        tt(sq[:].rearrange("p a (b n) -> p (a b) n", n=P), qk, qk, ALU.mult).then_inc(sem("sq_ready"), 1)
                        for l in range(LEVELS):
                            b = 1 << l
                            wait(pool, w, "h_exp", l - 1)
                            left = free_ap(hin[:, u, NG, :], 0, [[2 * b, HOP // (2 * b)], [HOP + b, 2], [1, b]])
                            mid = free_ap(hin[:, u, NG, :], b - 1, [[2 * b, HOP // (2 * b)], [HOP, 2], [0, b]])
                            out = dx[:, l % 2, :].rearrange("p (n a b) -> p n a b", a=2, b=b)
                            tt(out, left, mid, ALU.subtract).then_inc(sem("dx_ready"), 1)
                            if l == 0:
                                wait(pool, w, "m_e", 0)
                                tt(R[:], free_ap(keep["ident"][:], 0, [[0, V], [1, P]]), free_ap(keep["ident"][:], 0, [[0, V], [1, P]]),
                                   ALU.mult).then_inc(sem("r_init"), 1)
                        wait(pool, w, "h_exp", LEVELS - 1)
                        end = free_ap(hin[:, u, NG, :], last, [[P, H], [0, P]])
                        tt(dx[:, LEVELS % 2, :].rearrange("p (h n) -> p h n", n=P), hin[:, u, NG:NG + H, :], end, ALU.subtract).then_inc(sem("dx_ready"), 1)
                        wait(pool, w, "e_h", 1)
                        wait(pool, w, "m_ho", 0)
                        tt(qe[:].rearrange("p (h n) -> p h n", n=P), hin[:, u, QH:QH + H, :], egh[:], ALU.mult).then_inc(sem("qe_ready"), 1)
                        wait(pool, w, "qkn_ready", 2)
                        wait(pool, w, "e_g", 4)
                        wait(pool, w, "m_o", 0)
                        tt(qg[:].rearrange("p (a b) n -> p a b n", b=2), free_ap(qkn[:, 0, :], 0, [[P, Q], [0, 2], [1, P]]),
                           eg[:].rearrange("p (a b) n -> p a b n", b=2), ALU.mult).then_inc(sem("qg_ready"), 1)
                        wait(pool, w, "kt_ready", 1)
                        wait(pool, w, "cols_ready", 2)
                        wait(pool, w, "m_ds", 0)
                        tt(ks[:].rearrange("p (a b) n -> p a b n", b=2), free_ap(kt[:], 0, [[P, Q], [0, 2], [1, P]]),
                           free_ap(bk[:], 0, [[2, Q], [1, 2], [0, P]]), ALU.mult).then_inc(sem("ks_ready"), 1)
                        wait(pool, w, "h_exp", LEVELS + 1)
                        wait(pool, w, "m_hkt", 0)
                        tt(flat(ke), hin[:, u, KH:KH + H, :].rearrange("p h n -> p (h n)"), hx[:, LEVELS % 2, :], ALU.mult).then_inc(sem("ke_ready"), 1)

            @block.tensor
            def _(pe):
                credits(pe, "pe")
                mm, turn, ident = nc.tensor.matmul, nc.tensor.transpose, keep["ident"][:]
                pe.wait_ge(s_zero, 2)
                with pe.Fori(0, turns) as i:
                    for u in range(2):
                        w = i * 2 + u
                        def scores(l):
                            if l == 0:
                                pe.wait_ge(h_in[u], i * 16 + 16)
                                wait(pe, w, "t1h_ready", 0)
                            else:
                                wait(pe, w, "h_kq", l)
                                if l == 1:
                                    wait(pe, w, "rnh_ready", 0)
                                else:
                                    wait(pe, w, "h_pred", l - 1)
                            for h in range(H):
                                if l == 0:
                                    a, b = hin[:, u, KH + h, :], hin[:, u, QH + h, :]
                                else:
                                    a = b = kql[:, l % 2, h * P:(h + 1) * P]
                                x = mm(HB[l % 2][:, h, :], a, b, start=True, stop=True)
                            x.then_inc(sem("m_hs"), 1)

                        wait(pe, w, "sq_ready", 1)
                        wait(pe, w, "s_done", 0)
                        for g in range(2):
                            mm(M[g][:], keep["ones"][:], sq[:, g, :], start=True, stop=True).then_inc(sem("m_ssq"), 1)
                        wait(pe, w, "la_ready", 1)
                        wait(pe, w, "t1c_ready", 0)
                        for g in range(2):
                            mm(M[2 + g][:], keep["ones"][:], four(la_t, g), start=True, stop=True).then_inc(sem("m_g"), 1)
                        for g in range(2):
                            wait(pe, w, "rn_ready", 2 * g + 1)
                            mm(M[g][:], masks["later"][:], four(la_t, g), start=True, stop=True).then_inc(sem("m_g"), 1)
                        scores(0)
                        wait(pe, w, "rnc_ready", 0)
                        mm(G[0][:, 0, 0:V], masks["causal"][:], lbw[:, 0:V], start=True, stop=True)
                        mm(G[0][:, 0, V:2 * V], masks["later"][:], lbw[:, 0:V], start=True, stop=True).then_inc(sem("m_col"), 1)
                        pe.wait_ge(c_in[u], i * 16 + 16)
                        for g in range(2):
                            wait(pe, w, "e_g", g + 1)
                            for h in range(4):
                                x = turn(M[2 + g][:, h, :], cin[:, u, VC + 4 * g + h, :], ident)
                            x.then_inc(sem("m_vt"), 1)
                        scores(1)
                        wait(pe, w, "qkn_ready", 2)
                        for g in range(2):
                            wait(pe, w, "e_g", 3 + g)
                            for j in range(2):
                                q = 2 * g + j
                                x = mm(M[g][:, 2 * j:2 * j + 2, :], qkn[:, 1, q * P:(q + 1) * P],
                                       free_ap(qkn[:, 0, :], q * P, [[Q * P, 2], [1, P]]), start=True, stop=True)
                            x.then_inc(sem("m_kq"), 1)
                        for q in range(Q):
                            x = turn(G[1][:, q, :], qkn[:, 1, q * P:(q + 1) * P], ident)
                        x.then_inc(sem("m_kt"), 1)
                        for g in range(2):
                            if g == 0:
                                wait(pe, w, "e_col", 1)
                            else:
                                wait(pe, w, "kt_ready", 1)
                            wait(pe, w, "r_pair", g + 1)
                            for h in range(4):
                                x = turn(G[g][:, h, :], R[:, 4 * g + h, :], ident)
                            x.then_inc(sem("m_t"), 1)
                        def turn_hv():
                            wait(pe, w, "vt_ready", 2)
                            for h in range(H):
                                x = turn(M[2][:, h, :], hin[:, u, VH + h, :], ident)
                            x.then_inc(sem("m_hvt"), 1)

                        def product_ks(g):
                            wait(pe, w, "kqm_ready", g + 1)
                            for j in range(2):
                                q = 2 * g + j
                                x = mm(M[g][:, 2 * j:2 * j + 2, :], qkn[:, 1, q * P:(q + 1) * P], S[:, 2 * q:2 * q + 2, :], start=True, stop=True)
                            x.then_inc(sem("m_ks"), 1)

                        for l in range(1, LEVELS):
                            fin = l == LEVELS - 1
                            for g in range(2):
                                if l == 1:
                                    wait(pe, w, "t_ready", g + 1)
                                else:
                                    wait(pe, w, "t_pred", 2 * (l - 2) + g + 1)
                                    wait(pe, w, "r_ready", 2 * (l - 2) + g + 1)
                                for h in range(4 * g, 4 * g + 4):
                                    x = mm(G[g][:, h % 4, :], an[:, h, 1, :], TT[:, h, :], start=True, stop=True)
                                x.then_inc(sem("m_w"), 1)
                            if l == 1:
                                scores(2)
                            for g in range(2):
                                wait(pe, w, "w_ready", 2 * (l - 1) + g + 1)
                                for h in range(4 * g, 4 * g + 4):
                                    if fin:
                                        x = mm(G[g][:, h % 4, :], W[:, h, :], R[:, h, :], start=True, stop=True)
                                    else:
                                        x = mm(G[g][:, h % 4, :], R[:, h, :], W[:, h, :], start=True, stop=True)
                                x.then_inc(sem("m_z"), 1)
                            if not fin:
                                scores(2 + l)
                                for g in range(2):
                                    wait(pe, w, "t_pred", 2 * (l - 1) + g + 1)
                                    for h in range(4 * g, 4 * g + 4):
                                        x = turn(G[g][:, h % 4, :], TT[:, h, :], ident)
                                    x.then_inc(sem("m_r"), 1)
                            if l == 3:
                                turn_hv()
                            elif l in (4, 5):
                                product_ks(l - 4)
                        wait(pe, w, "ke_ready", 1)
                        for h in range(H):
                            x = turn(M[3][:, h, :], ke[:, h, :], ident)
                        x.then_inc(sem("m_hkt"), 1)
                        wait(pe, w, "qe_ready", 1)
                        wait(pe, w, "h_turned", 2)
                        wait(pe, w, "h_pred", 8)
                        for h in range(H):
                            mm(HB[0][:, h, :], SH[:, h, :], qe[:, h * P:(h + 1) * P], start=True, stop=False)
                            x = mm(HB[0][:, h, :], vht[:, h, :], A[:, h, :], start=False, stop=True)
                        x.then_inc(sem("m_ho"), 1)
                        for h in range(H):
                            x = mm(HB[1][:, h, :], kht[:, h, :], vht[:, h, :], start=True, stop=True)
                        x.then_inc(sem("m_hds"), 1)
                        for g in range(2):
                            wait(pe, w, "r_done", g + 1)
                            wait(pe, w, "res", 4 * g + 4)
                            for h in range(4 * g, 4 * g + 4):
                                x = mm(G[g][:, h % 4, :], R[:, h, :], r[:, h, :], start=True, stop=True)
                            x.then_inc(sem("m_e"), 1)
                        wait(pe, w, "qg_ready", 1)
                        for g in range(2):
                            wait(pe, w, "e_ready", g + 1)
                            for h in range(4 * g, 4 * g + 4):
                                mm(M[2 + g][:, h % 4, :], S[:, h, :], qg[:, h, :], start=True, stop=False)
                                x = mm(M[2 + g][:, h % 4, :], e[:, h, :], an[:, h, 0, :], start=False, stop=True)
                            x.then_inc(sem("m_o"), 1)
                        wait(pe, w, "ks_ready", 1)
                        for g in range(2):
                            for h in range(4 * g, 4 * g + 4):
                                x = mm(M[g][:, h % 4, :], ks[:, h, :], e[:, h, :], start=True, stop=True)
                            x.then_inc(sem("m_ds"), 1)
                        wait(pe, w, "hs_done", 4)
                        wait(pe, w, "sqh_ready", 1)
                        mm(HB[1][:], keep["ones"][:], sqh[:], start=True, stop=True).then_inc(sem("m_hn"), 1)
                        for g in range(2):
                            wait(pe, w, "sqc_ready", g + 1)
                            mm(G[g][:], keep["ones"][:], four(sqc, g), start=True, stop=True).then_inc(sem("m_n"), 1)

            @block.scalar
            def _(act):
                nc.scalar.preload_act_table_set(TABLES)
                credits(act, "act")
                fn, eps = nc.scalar.activation, keep["eps"][:, 0:1]
                with act.Fori(0, turns) as i:
                    for u in range(2):
                        w = i * 2 + u
                        wait(act, w, "qkn_ready", 0)
                        for g in range(2):
                            wait(act, w, "m_ssq", g + 1)
                            fn(rn[:, g, :], flat(M[g]), ACT.Ln, bias=eps).then_inc(sem("rn_ready"), 1)
                            wait(act, w, "rn_ready", 2 * g + 1)
                            fn(rn[:, g, :], rn[:, g, :], ACT.Exp, scale=NEG_HALF).then_inc(sem("rn_ready"), 1)
                        wait(act, w, "s_done", 0)
                        wait(act, w, "hs_done", 0)
                        wait(act, w, "qg_ready", 0)
                        wait(act, w, "ks_ready", 0)
                        for g in range(4):
                            wait(act, w, "m_g", g + 1)
                            fn(four((eg, dec)[g // 2], g % 2), M[(g + 2) % 4][:], ACT.Exp).then_inc(sem("e_g"), 1)
                        wait(act, w, "m_col", 1)
                        fn(ecol[:], G[0][:, 0, 0:2 * V], ACT.Exp).then_inc(sem("e_col"), 1)
                        act.wait_ge(h_in[u], i * 16 + 16)
                        fn(egh[:], hin[:, u, GG:GG + H, :], ACT.Exp).then_inc(sem("e_h"), 1)

                        def level_exp(l):
                            wait(act, w, "dx_ready", l + 1)
                            if l >= 2:
                                wait(act, w, "h_kq", l - 1)
                            fn(hx[:, l % 2, :], dx[:, l % 2, :], ACT.Exp).then_inc(sem("h_exp"), 1)

                        wait(act, w, "ke_ready", 0)
                        level_exp(0)
                        level_exp(1)
                        for g in range(2):
                            wait(act, w, "m_vt", g + 1)
                            fn(four(vt, g), M[2 + g][:], ACT.Copy).then_inc(sem("vt_ready"), 1)
                        wait(act, w, "m_kt", 1)
                        fn(kt[:], G[1][:], ACT.Copy).then_inc(sem("kt_ready"), 1)
                        for g in range(2):
                            wait(act, w, "m_t", g + 1)
                            fn(four(TT, g), G[g][:], ACT.Copy).then_inc(sem("t_ready"), 1)
                        for l in range(1, LEVELS):
                            for g in range(2):
                                wait(act, w, "m_w", 2 * (l - 1) + g + 1)
                                fn(four(W, g), G[g][:], ACT.Copy).then_inc(sem("w_ready"), 1)
                            level_exp(l + 1)
                            if l < LEVELS - 1:
                                for g in range(2):
                                    wait(act, w, "m_r", 2 * (l - 1) + g + 1)
                                    fn(four(R, g), G[g][:], ACT.Copy).then_inc(sem("r_ready"), 1)
                            if l == 3:
                                wait(act, w, "m_hvt", 1)
                                fn(vht[:], M[2][:], ACT.Copy).then_inc(sem("h_turned"), 1)
                        wait(act, w, "m_hkt", 1)
                        fn(kht[:], M[3][:], ACT.Copy).then_inc(sem("h_turned"), 1)
                        wait(act, w, "m_ho", 1)
                        fn(sqh[:], HB[0][:], ACT.Square).then_inc(sem("sqh_ready"), 1)
                        for g in range(2):
                            wait(act, w, "m_e", g + 1)
                            fn(four(e, g), G[g][:], ACT.Copy).then_inc(sem("e_ready"), 1)
                        for g in range(2):
                            wait(act, w, "m_o", g + 1)
                            fn(four(sqc, g), M[2 + g][:], ACT.Square).then_inc(sem("sqc_ready"), 1)
                        mean = 1.0 / P / P
                        wait(act, w, "y_c", 0)
                        wait(act, w, "m_hn", 1)
                        fn(rnh[:], HB[1][:], ACT.Ln, scale=mean, bias=eps).then_inc(sem("rnh_ready"), 1)
                        wait(act, w, "rnh_ready", 1)
                        fn(rnh[:], rnh[:], ACT.Exp, scale=NEG_HALF).then_inc(sem("rnh_ready"), 1)
                        for g in range(2):
                            wait(act, w, "m_n", g + 1)
                            fn(four(rnc, g), G[g][:], ACT.Ln, scale=mean, bias=eps).then_inc(sem("rnc_ready"), 1)
                            wait(act, w, "rnc_ready", 2 * g + 1)
                            fn(four(rnc, g), four(rnc, g), ACT.Exp, scale=NEG_HALF).then_inc(sem("rnc_ready"), 1)

            @block.vector
            def _(dve):
                credits(dve, "dve")
                tt, ts, stt, pred = nc.vector.tensor_tensor, nc.vector.tensor_scalar, nc.vector.scalar_tensor_tensor, nc.vector.copy_predicated
                nc.vector.memset(S[:], 0.0).then_inc(s_zero, 1)
                nc.vector.memset(SH[:], 0.0).then_inc(s_zero, 1)

                def over(mask, l, n):
                    return free_ap(mask[:, l, :], 0, [[0, n], [1, P]]).bitcast(I32)

                def log_a(w):
                    wait(dve, w, "an_ready", 0)
                    wait(dve, w, "cols_ready", 0)
                    wait(dve, w, "m_col", 0)
                    wait(dve, w, "m_g", 0)
                    nc.vector.tensor_copy(lbw[:], keep["ab"][:, bass.ds(w * 2 * V, 2 * V)]).then_inc(sem("lb"), 1)
                    wait(dve, w, "lb", 1)
                    tt(la_t[:], free_ap(masks["causal"][:], 0, [[0, V], [1, P]]), spread(lbw[:, 0:V], P), ALU.mult).then_inc(sem("la_ready"), 1)

                log_a(0)
                with dve.Fori(0, turns) as i:
                    for u in range(2):
                        w = i * 2 + u
                        wait(dve, w, "m_ho", 0)
                        wait(dve, w, "m_hs", 1)
                        tt(A[:], HB[0][:], free_ap(keep["ident"][:], 0, [[0, H], [1, P]]), ALU.mult).then_inc(sem("h_pred"), 1)
                        wait(dve, w, "e_col", 1)
                        ts(neg_eg[:], ecol[:, 0:V], -1.0, None, ALU.mult).then_inc(sem("cols_ready"), 1)
                        tt(bk[:], ecol[:, V:2 * V], lbw[:, V:2 * V], ALU.mult).then_inc(sem("cols_ready"), 1)
                        dve.wait_ge(c_in[u], i * 16 + 16)
                        for g in range(2):
                            wait(dve, w, "rn_ready", 2 * g + 2)
                            tt(qkn[:, g, :].rearrange("p (h n) -> p h n", n=P), cin[:, u, QC + Q * g:QC + Q * g + Q, :],
                               rn[:, g, :].rearrange("p (h n) -> p h n", n=P), ALU.mult).then_inc(sem("qkn_ready"), 1)

                        def level_kq(l):
                            b = 1 << l
                            wait(dve, w, "h_exp", l + 1)
                            wait(dve, w, "m_hs", l)
                            kq = free_ap(hin[:, u, KH, :], 0, [[2 * b, HOP // (2 * b)], [HOP + b, 2], [1, b]])
                            shape = lambda t: t[:, (l + 1) % 2, :].rearrange("p (n a b) -> p n a b", a=2, b=b)
                            tt(shape(kql), kq, hx[:, l % 2, :].rearrange("p (n a b) -> p n a b", a=2, b=b), ALU.mult).then_inc(sem("h_kq"), 1)

                        def level_pred(l):
                            wait(dve, w, "h_pred", l + 1)
                            wait_apart(dve, sem("m_hs"), sems["m_hs"][0].at(w, l + 2), passed)
                            pred(A[:], over(masks["upper"], l, H), HB[(l + 1) % 2][:]).then_inc(sem("h_pred"), 1)

                        level_kq(0)
                        for g in range(2):
                            wait(dve, w, "m_kq", g + 1)
                            tt(kqm[:, 2 * g:2 * g + 2, :], M[g][:].rearrange("p (a b) n -> p a (b n)", b=2),
                               free_ap(masks["pair"][:], 0, [[0, 2], [1, 2 * P]]), ALU.mult).then_inc(sem("kqm_ready"), 1)
                        wait(dve, w, "e_g", 4)
                        wait(dve, w, "r_init", 1)
                        for h in range(V):
                            if h % 4 == 0:
                                wait(dve, w, "kqm_ready", h // 4 + 1)
                            stt(an[:, h, :, :], kqm[:, h // 2, :].rearrange("p (a n) -> p a n", a=2), lbw[:, V + h:V + h + 1],
                                free_ap(dec[:, h, :], 0, [[0, 2], [1, P]]), ALU.mult, ALU.mult).then_inc(sem("an_ready"), 1)
                            if h % 4 == 3:
                                wait_apart(dve, sem("an_ready"), sems["an_ready"][0].at(w, h + 1), passed)
                                pred(four(R, h // 4), over(masks["upper"], 0, 4), an[:, h - 3:h + 1, 1, :]).then_inc(sem("r_pair"), 1)
                        level_kq(1)
                        level_pred(0)
                        for l in range(1, LEVELS):
                            fin = l == LEVELS - 1
                            if not fin:
                                level_kq(l + 1)
                            for g in range(2):
                                wait_apart(dve, sem("m_z"), sems["m_z"][0].at(w, 2 * (l - 1) + g + 1), passed)
                                if fin:
                                    pred(four(R, g), over(masks["upper"], l, 4), G[g][:]).then_inc(sem("r_done"), 1)
                                else:
                                    pred(four(TT, g), over(masks["lower"], l, 4), G[g][:]).then_inc(sem("t_pred"), 1)
                            if not fin:
                                level_pred(l)
                        level_pred(LEVELS - 1)
                        log_a(w + 1)
                        wait(dve, w, "vt_ready", 2)
                        for h in range(V):
                            if h % 4 == 0:
                                wait(dve, w, "m_ks", h // 4 + 1)
                            stt(r[:, h, :], M[h // 4][:, h % 4, :], neg_eg[:, h:h + 1], vt[:, h, :], ALU.mult, ALU.add).then_inc(sem("res"), 1)
                        wait(dve, w, "m_hds", 1)
                        for h in range(H):
                            stt(SH[:, h, :], SH[:, h, :], egh[:, h, last:P], HB[1][:, h, :], ALU.mult, ALU.add).then_inc(sem("hs_done"), 1)
                        for h in range(V):
                            if h % 4 == 0:
                                wait(dve, w, "m_ds", h // 4 + 1)
                            stt(S[:, h, :], S[:, h, :], eg[:, h, last:P], M[h // 4][:, h % 4, :], ALU.mult, ALU.add).then_inc(sem("s_done"), 1)
                        wait(dve, w, "y_c", 0)
                        stt(t1h[:], HB[0][:], hw[:, 0:1], hin[:, u, ZH:ZH + H, :], ALU.mult, ALU.mult).then_inc(sem("t1h_ready"), 1)
                        for g in range(2):
                            wait(dve, w, "sqc_ready", g + 1)
                            stt(four(t1c, g), M[2 + g][:], hw[:, 1:2], cin[:, u, ZC + 4 * g:ZC + 4 * g + 4, :], ALU.mult, ALU.mult).then_inc(sem("t1c_ready"), 1)
                        dve.wait_ge(yh_out[u], i * 16 + 16)
                        dve.wait_ge(yc_out[u], i * 16 + 16)
                        wait(dve, w, "rnh_ready", 2)
                        wait(dve, w, "t1h_ready", 1)
                        tt(yh[:, u, :, :], t1h[:], rnh[:], ALU.mult).then_inc(sem("y_h"), 1)
                        for g in range(2):
                            wait(dve, w, "rnc_ready", 2 * g + 2)
                            wait(dve, w, "t1c_ready", g + 1)
                            tt(yc[:, u, 4 * g:4 * g + 4, :], four(t1c, g), four(rnc, g), ALU.mult).then_inc(sem("y_c"), 1)




def merge(nc, dm, io, keep, h_dram, y_dram, out):
    rows, K, T = vector_rows(dm), dm.kt, dm.blk
    D = dm.d // P
    NX = K + dm.wa + dm.hh + dm.vh
    KINDS = 5
    UD, U = KINDS * D, KINDS * D + D
    CH = 2
    WB = BLK // P
    assert dm.wa + dm.hh == K and dm.vh == K and D == K
    hd, yd = h_dram.rearrange("k p n -> p k n"), y_dram.rearrange("k p n -> p k n")
    with ExitStack() as c:
        sb = lambda n, s, d=F32: c.enter_context(nc.sbuf_tensor(n, s, d))
        xs = sb("xs", [P, 2, CH, BLK])
        xh, xl = sb("xh", [P, NX, BLK], F32R), sb("xl", [P, NX, BLK], F32R)
        stage = sb("wo_stage", [P, 2, K, P])
        wh, wl = sb("wo_high", [P, 2, K, P], F32R), sb("wo_low", [P, 2, K, P], F32R)
        sg = sb("sg", [P, 3, BLK])
        tmp = sb("tmp", [P, 2, BLK])
        mh, ml = sb("mh", [P, D, BLK], F32R), sb("ml", [P, D, BLK], F32R)
        ot = sb("ot", [P, D, BLK])
        xw = sb("xw", [P, 2, dm.d])
        fw = sb("fw", [P, dm.d])
        st = sb("st", [P, 2, 3])
        B = [c.enter_context(nc.psum_tensor(f"b_o{i}", [P, BLK], F32)) for i in range(8)]
        sem = lambda n: c.enter_context(nc.semaphore("m_" + n))
        w_in = [sem(f"w_in{s}") for s in range(2)]
        w_high, w_ready, unit_done = Ahead(sem("w_high"), 1), Ahead(sem("w_ready"), 1, 2), Ahead(sem("unit_done"), 1, 2)
        x_in = [sem(f"x_in{s}") for s in range(2)]
        x_high, x_ready = Ahead(sem("x_high"), NX // CH), Ahead(sem("x_ready"), NX // CH)
        gate, prod, summed = Ahead(sem("gate"), 3), Ahead(sem("prod"), 3), Ahead(sem("summed"), 2)
        m_high, merged = Ahead(sem("m_high"), 1), Ahead(sem("merged"), D)
        o_ready, turned, added = Ahead(sem("o_ready"), D), Ahead(sem("turned"), WB), Ahead(sem("added"), 2 * WB)
        stat, out_ready = Ahead(sem("stat"), 3 * WB), Ahead(sem("out_ready"), WB)
        xw_in, xw_out = [sem(f"xw_in{s}") for s in range(2)], [sem(f"xw_out{s}") for s in range(2)]
        fw_in, passed, passed_pe = sem("fw_in"), sem("passed"), sem("passed_pe")
        loads = [sum(2 if j % KINDS == 3 else 1 for j in range(m % 2, m + 1, 2)) for m in range(2 * KINDS)]
        per_pair = loads[-1]
        assert loads[-2] == per_pair
        per_block = per_pair * (D // 2) + D // 2

        def unit_no(tb, dp, m):
            return tb * U + (dp * (2 * KINDS) + m)

        with nc.Block() as block:
            @block.sync
            def _(sp):
                fnw = io["final_norm_w"]
                sp.dma_start(fw[:], bass.AP(fnw.tensor, 0, [[0, P], [1, dm.d]])).then_inc(fw_in, 16)
                for s in range(2):
                    sp.sem_inc(xw_out[s], 16)

                def load_w(tb, dp, m):
                    wait_apart(sp, w_ready.sem, w_ready.at(unit_no(tb, dp, m), -1), passed)
                    kind, cut = m % KINDS, bass.ds(dp * (2 * P) + (m // KINDS) * P, P)
                    slot = stage[:, m % 2, :, :]
                    view = lambda t: t.rearrange("(k p) c -> p k c", p=P)
                    if kind < 3:
                        sp.dma_start(slot, view(io["w_in"][0, :, bass.ds(dp * (2 * P) + (dm.gates + kind * dm.d + (m // KINDS) * P), P)])).then_inc(w_in[m % 2], 16)
                    elif kind == 3:
                        sp.dma_start(slot[:, 0:dm.wa, :], view(io["w_out_a"][0, :, cut])).then_inc(w_in[m % 2], 16)
                        sp.dma_start(slot[:, dm.wa:K, :], view(io["w_out_b"][0, :, cut])).then_inc(w_in[m % 2], 16)
                    else:
                        sp.dma_start(slot, view(io["w_out_c"][0, :, cut])).then_inc(w_in[m % 2], 16)

                def load_x(tb, k):
                    wait_apart(sp, x_ready.sem, x_ready.at(tb, k - 1), passed)
                    cut = bass.ds(tb * BLK, BLK)
                    src = hd[:, CH * k:CH * k + CH, cut] if CH * k < K else yd[:, CH * k - K:CH * k - K + CH, cut]
                    sp.dma_start(xs[:, k % 2, :, :], src).then_inc(x_in[k % 2], 16)

                def load_xw(tb, t):
                    wait_apart(sp, xw_out[t % 2], tb * (8 * WB) + (16 * (t // 2) + 16), passed)
                    sp.dma_start(xw[:, t % 2, :], io["x"][0, bass.ds(tb * BLK + t * P, P), :]).then_inc(xw_in[t % 2], 16)

                with sp.Fori(0, T) as tb:
                    for k in range(NX // CH):
                        load_x(tb, k)
                        if k % 2:
                            load_w(tb, 0, k // 2)
                    for m in range(NX // CH // 2, 2 * KINDS):
                        load_w(tb, 0, m)
                    with sp.Fori(1, D // 2) as dp:
                        for m in range(2 * KINDS):
                            load_w(tb, dp, m)
                    for t in range(2):
                        load_xw(tb, t)
                    with sp.Fori(0, D // 2) as ep:
                        for s in range(2):
                            wait_apart(sp, w_ready.sem, w_ready.at(tb * U + (ep * 2 + (UD + s)), -1), passed)
                            sp.dma_start(stage[:, s, :, :], io["w_o"][0, :, bass.ds(ep * (2 * P) + s * P, P)].rearrange("(k p) c -> p k c", p=P)
                                         ).then_inc(w_in[s], 16)
                    for t in range(WB):
                        wait_apart(sp, out_ready.sem, out_ready.at(tb, t + 1), passed)
                        sp.dma_start(out[0, bass.ds(tb * BLK + t * P, P), :], xw[:, t % 2, :]).then_inc(xw_out[t % 2], 16)
                        if t + 2 < WB:
                            load_xw(tb, t + 2)
                for s in range(2):
                    sp.wait_ge(xw_out[s], 8 * WB * T + 16)

            @block.gpsimd
            def _(pool):
                w_ready.credit(pool)
                with pool.Fori(0, T * U // 2) as i:
                    for s in range(2):
                        n = i * 2 + s
                        pool.wait_ge(w_high.sem, w_high.at(n, 1))
                        nc.gpsimd.tensor_tensor(wl[:, s, :, :], stage[:, s, :, :], wh[:, s, :, :].bitcast(F32), ALU.subtract).then_inc(w_ready.sem, 1)

            @block.tensor
            def _(pe):
                unit_done.credit(pe)
                turned.credit(pe)

                def product(bank, slot, ks, moving, first):
                    high, low = moving
                    for i, k in enumerate(ks):
                        for a, (w, x) in enumerate(((wh, high), (wl, high), (wh, low))):
                            x_ = nc.tensor.matmul(bank[:], w[:, slot, k, :], x[:, first + i, :], start=(i == 0 and a == 0),
                                                  stop=(i == len(ks) - 1 and a == 2))
                    return x_

                with pe.Fori(0, T) as tb:
                    with pe.Fori(0, D // 2) as dp:
                        for m in range(2 * KINDS):
                            kind, slot, tile = m % KINDS, m % 2, tb * D + (dp * 2 + m // KINDS)
                            pe.wait_ge(w_ready.sem, w_ready.at(unit_no(tb, dp, m), 1))
                            pe.wait_ge(x_ready.sem, x_ready.at(tb, (K, 2 * K, 3 * K)[max(kind - 2, 0)] // CH))
                            pe.wait_ge(added.sem, added.at(tb, 0))
                            if kind < 3:
                                pe.wait_ge(gate.sem, gate.at(tile, kind - 2))
                                last = product(B[kind], slot, range(K), (xh, xl), 0)
                            elif kind == 3:
                                pe.wait_ge(prod.sem, prod.at(tile, -1))
                                product(B[3], slot, range(dm.wa), (xh, xl), K)
                                last = product(B[4], slot, range(dm.wa, K), (xh, xl), K + dm.wa)
                            else:
                                pe.wait_ge(prod.sem, prod.at(tile, 0))
                                last = product(B[5], slot, range(K), (xh, xl), 2 * K)
                            last.then_inc(unit_done.sem, 1)
                    wait_apart(pe, merged.sem, merged.at(tb, D), passed_pe)
                    with pe.Fori(0, D // 2) as ep:
                        for s in range(2):
                            pe.wait_ge(w_ready.sem, w_ready.at(tb * U + (ep * 2 + (UD + s)), 1))
                            pe.wait_ge(o_ready.sem, ep * 2 + (tb * D + (D + s - 1)))
                            product(B[6 + s], s, range(K), (mh, ml), 0).then_inc(unit_done.sem, 1)
                    pe.wait_ge(o_ready.sem, o_ready.at(tb, D))
                    pe.wait_ge(gate.sem, gate.at(tb * D + D, 0))
                    pe.wait_ge(prod.sem, prod.at(tb * D + D, 0))
                    for t in range(WB):
                        if t >= 2:
                            pe.wait_ge(added.sem, added.at(tb, 2 * (t - 1)))
                        for e in range(D):
                            x_ = nc.tensor.transpose(B[2 * (t % 2) + e // 4][:, (e % 4) * P:(e % 4 + 1) * P], ot[:, e, t * P:(t + 1) * P], keep["ident"][:])
                        x_.then_inc(turned.sem, 1)

            @block.scalar
            def _(act):
                for s in (w_high, gate, o_ready, stat):
                    s.credit(act)

                def split(tb, n, slot, value):
                    act.wait_ge(w_in[slot], value)
                    act.wait_ge(unit_done.sem, unit_done.at(n, -1))
                    nc.scalar.activation(wh[:, slot, :, :], stage[:, slot, :, :], ACT.Copy).then_inc(w_high.sem, 1)

                with act.Fori(0, T) as tb:
                    nc.scalar.preload_act_table_set(SIGMOID_TABLES)
                    block_loads = tb * (16 * per_block)
                    split(tb, unit_no(tb, 0, 0), 0, block_loads + 16 * loads[0])
                    with act.Fori(0, D // 2) as dp:
                        for m in range(2 * KINDS):
                            n, tile = unit_no(tb, dp, m), tb * D + (dp * 2 + m // KINDS)
                            pair_loads = block_loads + dp * (16 * per_pair)
                            split(tb, n + 1, (m + 1) % 2, pair_loads + (16 * loads[m + 1] if m + 1 < 2 * KINDS else 16 * per_pair + 16))
                            if m % KINDS < 3:
                                act.wait_ge(unit_done.sem, unit_done.at(n, 1))
                                act.wait_ge(prod.sem, prod.at(tile, 0))
                                at = dp * 2 + (rows["b_gate"] + (m % KINDS) * D + m // KINDS)
                                nc.scalar.activation(sg[:, m % KINDS, :], B[m % KINDS][:], ACT.Sigmoid,
                                                     bias=keep["cols"][:, bass.ds(at, 1)]).then_inc(gate.sem, 1)
                    all_pairs = 16 * per_pair * (D // 2)

                    def out_tile(ep, s, more):
                        n = tb * U + (ep * 2 + (UD + s))
                        if more:
                            split(tb, n + 1, 1 - s, block_loads + ep * 16 + (all_pairs + 16 * (1 + s)))
                        act.wait_ge(unit_done.sem, unit_done.at(n, 1))
                        act.wait_ge(turned.sem, turned.at(tb, 0))
                        nc.scalar.activation(ot[:, bass.ds(ep * 2 + s, 1), :], B[6 + s][:], ACT.Copy).then_inc(o_ready.sem, 1)

                    with act.Fori(0, D // 2 - 1) as ep:
                        for s in range(2):
                            out_tile(ep, s, True)
                    out_tile(D // 2 - 1, 0, True)
                    out_tile(D // 2 - 1, 1, False)
                    nc.scalar.preload_act_table_set(TABLES)
                    for t in range(WB):
                        s = t % 2
                        act.wait_ge(added.sem, added.at(tb, 2 * t + 2))
                        nc.scalar.activation(tmp[:].rearrange("p a n -> p (a n)"), xw[:, s, :], ACT.Square, accum_out=st[:, s, 0:1]).then_inc(stat.sem, 1)
                        act.wait_ge(stat.sem, stat.at(tb, 3 * t + 1))
                        nc.scalar.activation(st[:, s, 1:2], st[:, s, 0:1], ACT.Ln, scale=1.0 / dm.d, bias=keep["eps"][:, 0:1]).then_inc(stat.sem, 1)
                        act.wait_ge(stat.sem, stat.at(tb, 3 * t + 2))
                        nc.scalar.activation(st[:, s, 2:3], st[:, s, 1:2], ACT.Exp, scale=NEG_HALF).then_inc(stat.sem, 1)

            @block.vector
            def _(dve):
                for s in (x_high, x_ready, prod, summed, m_high, merged, added, out_ready):
                    s.credit(dve)
                tt, ts = nc.vector.tensor_tensor, nc.vector.tensor_scalar
                dve.wait_ge(fw_in, 16)
                with dve.Fori(0, T) as tb:
                    for k in range(NX // CH):
                        dve.wait_ge(x_in[k % 2], tb * (16 * (NX // CH // 2)) + (16 * (k // 2) + 16))
                        cut = slice(CH * k, CH * k + CH)
                        ts(xh[:, cut, :], xs[:, k % 2, :, :], 1.0, None, ALU.mult).then_inc(x_high.sem, 1)
                        dve.wait_ge(x_high.sem, x_high.at(tb, k + 1))
                        tt(xl[:, cut, :], xs[:, k % 2, :, :], xh[:, cut, :].bitcast(F32), ALU.subtract).then_inc(x_ready.sem, 1)
                    with dve.Fori(0, D // 2) as dp:
                        for dd in range(2):
                            tile = tb * D + (dp * 2 + dd)
                            ab = unit_no(tb, dp, KINDS * dd + 3)
                            dve.wait_ge(gate.sem, gate.at(tile, 3))
                            dve.wait_ge(unit_done.sem, unit_done.at(ab, 1))
                            dve.wait_ge(merged.sem, merged.at(tb, 0) + (dp * 2 + dd))
                            tt(tmp[:, 0, :], B[3][:], sg[:, 0, :], ALU.mult).then_inc(prod.sem, 1)
                            tt(tmp[:, 1, :], B[4][:], sg[:, 1, :], ALU.mult).then_inc(prod.sem, 1)
                            dve.wait_ge(prod.sem, prod.at(tile, 2))
                            tt(tmp[:, 0, :], tmp[:, 0, :], tmp[:, 1, :], ALU.add).then_inc(summed.sem, 1)
                            dve.wait_ge(unit_done.sem, unit_done.at(ab, 2))
                            dve.wait_ge(summed.sem, summed.at(tile, 1))
                            tt(tmp[:, 1, :], B[5][:], sg[:, 2, :], ALU.mult).then_inc(prod.sem, 1)
                            dve.wait_ge(prod.sem, prod.at(tile, 3))
                            tt(tmp[:, 0, :], tmp[:, 0, :], tmp[:, 1, :], ALU.add).then_inc(summed.sem, 1)
                            dve.wait_ge(summed.sem, summed.at(tile, 2))
                            at = bass.ds(dp * 2 + dd, 1)
                            ts(mh[:, at, :], tmp[:, 0:1, :], 1.0, None, ALU.mult).then_inc(m_high.sem, 1)
                            dve.wait_ge(m_high.sem, m_high.at(tile, 1))
                            tt(ml[:, at, :], tmp[:, 0:1, :], mh[:, at, :].bitcast(F32), ALU.subtract).then_inc(merged.sem, 1)
                    for t in range(WB):
                        s = t % 2
                        dve.wait_ge(turned.sem, turned.at(tb, t + 1))
                        dve.wait_ge(xw_in[s], tb * (8 * WB) + (16 * (t // 2) + 16))
                        for b in range(2):
                            half = xw[:, s, b * BLK:(b + 1) * BLK]
                            tt(half, B[2 * s + b][:], half, ALU.add).then_inc(added.sem, 1)
                        dve.wait_ge(stat.sem, stat.at(tb, 3 * t + 3))
                        nc.vector.scalar_tensor_tensor(xw[:, s, :], xw[:, s, :], st[:, s, 2:3], fw[:], ALU.mult, ALU.mult).then_inc(out_ready.sem, 1)


def hybrid_trunk(nc, io, out):
    dm = Dims(io["x"], io["w_in"], io["w_out_a"], io["w_out_b"], io["w_out_c"])
    h_dram = nc.dram_tensor("h_scratch", [dm.kt, P, dm.seq], F32).ap()
    s_dram = nc.dram_tensor("branch_scratch", [branch_tiles(dm)["end"], P, dm.seq], F32).ap()
    y_dram = nc.dram_tensor("y_scratch", [dm.wa + dm.hh + dm.vh, P, dm.seq], F32).ap()
    with ExitStack() as c:
        sb = lambda n, s, d=F32: c.enter_context(nc.sbuf_tensor(n, s, d))
        keep = {"ident": sb("ident", [P, P]), "ones": sb("ones", [P, P]), "cols": sb("cols", [P, P]),
                "eps": sb("eps", [P, 1]), "a_log": sb("a_log_t", [P, dm.vh]), "dt_bias": sb("dt_bias_t", [P, dm.vh]),
                "lb": sb("lb", [P, dm.hh]), "one_less_lb": sb("one_less_lb", [P, dm.hh]), "head_w": sb("head_w", [P, 2]),
                "ab": sb("ab", [P, (dm.win + 1) * 2 * dm.vh])}
        constants(nc, dm, io, keep)
        with nc.sbuf_tensor("hh", [P, dm.kt, dm.seq], F32R) as hh, nc.sbuf_tensor("hl", [P, dm.kt, dm.seq], F32R) as hl:
            norm_and_transpose(nc, dm, io, keep, hh, hl, h_dram)
            project(nc, dm, io, keep, hh, hl, s_dram, y_dram)
        recur(nc, dm, keep, s_dram, y_dram)
        merge(nc, dm, io, keep, h_dram, y_dram, out)


_INS = ["x", "norm_w", "w_in", "b_gate", "conv_a", "conv_c", "a_log", "dt_bias", "lower_bounds",
        "hgrn_norm_w", "gdn_norm_w", "w_out_a", "w_out_b", "w_out_c", "w_o", "final_norm_w"]


def kernel(**inputs):
    import numpy as _np
    import concourse.bacc as _bacc
    from concourse import mybir as _mybir
    from concourse.bass_utils import run_bass_kernel_spmd as _run

    nc = _bacc.Bacc("TRN2", target_bir_lowering=False, num_devices=1)
    arrays, io = {}, {}
    for name in _INS:
        a = _np.ascontiguousarray(inputs[name])
        arrays[f"in_{name}_dram"] = a
        io[name] = nc.dram_tensor(f"in_{name}_dram", a.shape, _mybir.dt.from_np(a.dtype), kind="ExternalInput").ap()
    out = nc.dram_tensor("out_0_dram", inputs["x"].shape, _mybir.dt.float32, kind="ExternalOutput").ap()
    hybrid_trunk(nc, io, out)
    r = _run(nc, [arrays], core_ids=[0])
    return r.results[0]["out_0_dram"]
```

```python
from contextlib import ExitStack

import concourse.bass as bass
from concourse import mybir

F32 = mybir.dt.float32
F32R = mybir.dt.float32r
I32 = mybir.dt.int32
ALU = mybir.AluOpType
ACT = mybir.ActivationFunctionType

P = 128
LEVELS = P.bit_length() - 1
BLK = 512
EPS = 1e-6
MIN_F = 1e-30
F_SPLIT = 2.0 ** -60
NEG_HALF = -0.5
TABLES = "natural_log_exp_and_others"
SILU_TABLES = "silu_and_others"
SIGMOID_TABLES = "sigmoid_and_others"


class Dims:

    def __init__(self, x, w_in, w_out_a, w_out_b, w_out_c):
        self.seq, self.d = x.shape[1], x.shape[2]
        self.cols = w_in.shape[2]
        self.kt = self.d // P
        self.wa = w_out_a.shape[1] // P
        self.hh = w_out_b.shape[1] // P
        self.vh = w_out_c.shape[1] // P
        self.qh = self.vh // 2
        self.win = self.seq // P
        self.blk = self.seq // BLK
        widths = [self.wa] * 4 + [self.hh] * 4 + [self.qh, self.qh, self.vh]
        at = [0]
        for n in widths:
            at.append(at[-1] + n * P)
        (self.a_b, self.a_c, self.a_x, self.a_z, self.b_q, self.b_f, self.b_i, self.b_z,
         self.c_q, self.c_k, self.c_v, self.c_beta) = at
        self.c_z = self.c_beta + 2 * self.vh
        self.gates = self.c_z + self.vh * P
        assert self.gates + 3 * self.d == self.cols


class Ahead:

    def __init__(self, sem, per, turns=1):
        self.sem, self.per, self.turns = sem, per, turns

    def credit(self, engine):
        engine.sem_inc(self.sem, self.per * self.turns)

    def at(self, turn, k):
        return turn * self.per + (self.per * self.turns + k)


def wait_apart(engine, sem, value, passed):
    engine.wait_ge(sem, value)
    engine.sem_inc(passed, 1)


def free_ap(ap, offset, dims):
    return bass.AP(ap.tensor, ap.offset + offset, [list(ap.ap[0])] + [list(x) for x in dims])


def across(ap, n):
    return free_ap(ap, 0, [[0, n], [1, ap.shape[-1]]])


def spread(ap, n):
    return free_ap(ap, 0, [[ap.ap[-1][0], ap.shape[-1]], [0, n]])


def vector_rows(dm):
    rows, at = {}, 0
    for name, n in (("norm_w", dm.kt), ("b_gate", 3 * dm.kt), ("conv_a", 3 * dm.wa),
                    ("conv_c", 4 * (2 * dm.qh + dm.vh)), ("lower", dm.hh), ("hgrn_w", 1), ("gdn_w", 1)):
        rows[name] = at
        at += n
    rows["end"] = at
    assert at <= P
    return rows


def fill_masks(pool, masks, ones, cut):
    set_to = []
    for name, mask in masks.items():
        if name == "pair":
            set_to += [(mask[:, 0, :], 1.0), (mask[:, 1, :], -1.0)]
        else:
            set_to.append((mask[:], 0.0 if name in ("upper", "lower") else 1.0))
    for ap, value in set_to:
        pool.memset(ap, value).then_inc(ones, 1)
    n_set = len(set_to)
    pool.wait_ge(ones, n_set)
    n = 0

    def half(mask, l, right):
        b = 1 << l
        return free_ap(mask[:, l, :], b if right else 0, [[2 * b, P // (2 * b)], [1, b]])

    def select(ap, op, base, pattern, by):
        nonlocal n
        n += 1
        pool.affine_select(out=ap, in_=ap, compare_op=op, fill=0.0, base=base, pattern=pattern,
                           channel_multiplier=by).then_inc(cut, 1)
        pool.wait_ge(cut, n)

    if "causal" in masks:
        select(masks["causal"][:], ALU.is_ge, 0, [[1, P]], -1)
    if "later" in masks:
        select(masks["later"][:], ALU.is_gt, 0, [[-1, P]], 1)
    if "pair" in masks:
        select(masks["pair"][:, 0, :], ALU.is_ge, 0, [[1, P]], -1)
        select(masks["pair"][:, 1, :], ALU.is_gt, 0, [[1, P]], -1)
    for name, right in (("upper", True), ("lower", False)):
        if name in masks:
            levels = masks[name].shape[1]
            for l in range(levels):
                pool.memset(half(masks[name], l, right), 1.0).then_inc(ones, 1)
            n_set += levels
            pool.wait_ge(ones, n_set)
            for l in range(levels):
                b = 1 << l
                blocks = P // (2 * b)
                first = 0 if right else b
                ap = half(masks[name], l, right)
                select(ap, ALU.is_ge, -first, [[-2 * b, blocks], [0, b]], 1)
                select(ap, ALU.is_ge, first + b - 1, [[2 * b, blocks], [0, b]], -1)
    return n


def constants(nc, dm, io, keep):
    rows = vector_rows(dm)
    n = rows["end"]
    with ExitStack() as c:
        vec = c.enter_context(nc.sbuf_tensor("vec", [P, P], F32))
        low = c.enter_context(nc.sbuf_tensor("low", [P, 4, dm.hh], F32))
        ps = c.enter_context(nc.psum_tensor("ps_vec", [P, P], F32))
        S = {k: c.enter_context(nc.semaphore("c_" + k)) for k in "loaded made turned copied low_exp low gave".split()}
        ident, ones, cols, eps = keep["ident"], keep["ones"], keep["cols"], keep["eps"]
        sources = [("norm_w", io["norm_w"].rearrange("l (r c) -> (l r) c", c=P)),
                   ("b_gate", io["b_gate"].rearrange("l (r c) -> (l r) c", c=P)),
                   ("conv_a", io["conv_a"].rearrange("l i (r c) -> (l i r) c", c=P)),
                   ("conv_c", io["conv_c"].rearrange("l i (r c) -> (l i r) c", c=P)),
                   ("lower", io["lower_bounds"].rearrange("l (r c) -> (l r) c", c=P)),
                   ("hgrn_w", io["hgrn_norm_w"]), ("gdn_w", io["gdn_norm_w"])]
        with nc.Block() as block:
            @block.sync
            def _(sp):
                for name, src in sources:
                    sp.dma_start(vec[rows[name]:rows[name] + src.shape[0], :], src).then_inc(S["loaded"], 16)
                for name, dst in (("a_log", keep["a_log"]), ("dt_bias", keep["dt_bias"])):
                    src = io[name]
                    sp.dma_start(dst[:], bass.AP(src.tensor, 0, [[0, P], [1, dm.vh]])).then_inc(S["loaded"], 16)
                sp.wait_ge(S["loaded"], 16 * (len(sources) + 2))

            @block.gpsimd
            def _(pool):
                pool.memset(ident[:], 0.0).then_inc(S["made"], 1)
                pool.memset(ones[:], 1.0).then_inc(S["made"], 1)
                pool.memset(eps[:], EPS).then_inc(S["made"], 1)
                pool.wait_ge(S["made"], 3)
                pool.affine_select(out=ident[:], in_=ident[:], compare_op=ALU.not_equal, fill=1.0, base=0,
                                   pattern=[[-1, P]], channel_multiplier=1).then_inc(S["made"], 1)

            @block.tensor
            def _(pe):
                pe.wait_ge(S["made"], 4)
                pe.wait_ge(S["loaded"], 16 * (len(sources) + 2))
                nc.tensor.transpose(ps[:, 0:n], vec[0:n, :], ident[0:n, 0:n]).then_inc(S["turned"], 1)

            @block.scalar
            def _(act):
                nc.scalar.preload_act_table_set(TABLES)
                act.wait_ge(S["low"], 1)
                nc.scalar.activation(low[:, 1, :], low[:, 0, :], ACT.Exp).then_inc(S["low_exp"], 1)

            @block.vector
            def _(dve):
                dve.wait_ge(S["turned"], 1)
                nc.vector.tensor_copy(cols[:, 0:n], ps[:, 0:n]).then_inc(S["copied"], 1)
                dve.wait_ge(S["copied"], 1)
                lw = cols[:, rows["lower"]:rows["lower"] + dm.hh]
                nc.vector.tensor_tensor(low[:, 0, :], lw, lw, ALU.subtract).then_inc(S["low"], 1)
                dve.wait_ge(S["low_exp"], 1)
                nc.vector.reciprocal(low[:, 2, :], low[:, 1, :]).then_inc(S["low"], 1)
                dve.wait_ge(S["low"], 2)
                nc.vector.tensor_tensor(low[:, 3, :], low[:, 1, :], low[:, 2, :], ALU.mult).then_inc(S["low"], 1)
                dve.wait_ge(S["low"], 3)
                nc.vector.tensor_tensor(keep["lb"][:], low[:, 3, :], low[:, 3, :], ALU.subtract).then_inc(S["low"], 1)
                dve.wait_ge(S["low"], 4)
                nc.vector.tensor_scalar(keep["one_less_lb"][:], keep["lb"][:], -1.0, 1.0, ALU.mult, ALU.add).then_inc(S["low"], 1)
                for k, name in enumerate(("hgrn_w", "gdn_w")):
                    nc.vector.tensor_scalar(keep["head_w"][:, k:k + 1], cols[:, rows[name]:rows[name] + 1], float(P) ** -0.5,
                                            None, ALU.mult).then_inc(S["low"], 1)


def norm_and_transpose(nc, dm, io, keep, hh, hl, h_dram):
    rows = vector_rows(dm)
    K, V = dm.kt, dm.vh
    with ExitStack() as c:
        sb = lambda n, s, d=F32: c.enter_context(nc.sbuf_tensor(n, s, d))
        xin, xn = sb("xin", [P, 2, dm.d]), sb("xn", [P, 2, dm.d])
        ht = sb("ht", [P, 2, K, P])
        wsm = sb("wsm", [P, K, 2 * V])
        stat = sb("stat", [P, 2, 3])
        z = sb("z", [P, 6, dm.win * V])
        ps = [c.enter_context(nc.psum_tensor(f"ps_h{i}", [P, BLK], F32)) for i in range(6)]
        sem = lambda n: c.enter_context(nc.semaphore("n_" + n))
        x_in = [Ahead(sem(f"x_in{u}"), 16) for u in range(2)]
        h_out = [Ahead(sem(f"h_out{u}"), 16) for u in range(2)]
        squared, rstd, scaled, turned = Ahead(sem("squared"), 1), Ahead(sem("rstd"), 2), Ahead(sem("scaled"), 1), Ahead(sem("turned"), 1, 2)
        weighted, high, low, small, kept = Ahead(sem("weighted"), 2, 2), Ahead(sem("high"), 1), Ahead(sem("low"), 1, 2), Ahead(sem("small"), 1, 2), Ahead(sem("kept"), 1, 2)
        w_in, passed = sem("w_in"), sem("passed")
        tail_v, tail_a = sem("tail_v"), sem("tail_a")
        turns = dm.win // 2
        nw = keep["cols"][:, rows["norm_w"]:rows["norm_w"] + K]
        hd = h_dram.rearrange("k p n -> p k n")
        with nc.Block() as block:
            @block.sync
            def _(sp):
                sp.dma_start(wsm[:], io["w_in"][0, :, dm.c_beta:dm.c_beta + 2 * V].rearrange("(k p) c -> p k c", p=P)).then_inc(w_in, 16)
                for u in range(2):
                    h_out[u].credit(sp)

                def load_pair(i):
                    for u in range(2):
                        wait_apart(sp, scaled.sem, i * 2 + (u + 1), passed)
                        sp.dma_start(xin[:, u, :], io["x"][0, bass.ds((i * 2 + u) * P, P), :]).then_inc(x_in[u].sem, 16)

                def store_pair(i):
                    for u in range(2):
                        w = i * 2 + u
                        wait_apart(sp, weighted.sem, weighted.at(w, 2), passed)
                        sp.dma_start(hd[:, :, bass.ds(w * P, P)], ht[:, u, :, :]).then_inc(h_out[u].sem, 16)

                load_pair(0)
                with sp.Fori(0, turns - 1) as i:
                    load_pair(i + 1)
                    store_pair(i)
                store_pair(turns - 1)
                for u in range(2):
                    sp.wait_ge(h_out[u].sem, 16 * turns + 16)
                sp.wait_ge(w_in, 16)

            @block.scalar
            def _(act):
                nc.scalar.preload_act_table_set(TABLES)
                for t in (squared, rstd, high):
                    t.credit(act)

                def statistics(i, u):
                    w = i * 2 + u
                    act.wait_ge(x_in[u].sem, i * 16 + 16)
                    act.wait_ge(scaled.sem, w + 1)
                    act.wait_ge(turned.sem, turned.at(w, -1))
                    nc.scalar.activation(xn[:, u, :], xin[:, u, :], ACT.Square, accum_out=stat[:, u, 0:1]).then_inc(squared.sem, 1)
                    act.wait_ge(squared.sem, squared.at(w, 1))
                    nc.scalar.activation(stat[:, u, 1:2], stat[:, u, 0:1], ACT.Ln, scale=1.0 / dm.d, bias=keep["eps"][:, 0:1]).then_inc(rstd.sem, 1)
                    act.wait_ge(rstd.sem, rstd.at(w, 1))
                    nc.scalar.activation(stat[:, u, 2:3], stat[:, u, 1:2], ACT.Exp, scale=NEG_HALF).then_inc(rstd.sem, 1)

                def high_part(w, u):
                    act.wait_ge(weighted.sem, weighted.at(w, 2))
                    nc.scalar.activation(hh[:, :, bass.ds(w * P, P)], ht[:, u, :, :], ACT.Copy).then_inc(high.sem, 1)

                for u in range(2):
                    statistics(0, u)
                with act.Fori(0, turns - 1) as i:
                    for u in range(2):
                        statistics(i + 1, u)
                        high_part(i * 2 + u, u)
                for u in range(2):
                    high_part(dm.win - 2 + u, u)
                act.wait_ge(tail_v, 3)
                nc.scalar.activation(z[:, 1, :], z[:, 0, :], ACT.Exp, scale=-1.0).then_inc(tail_a, 1)
                nc.scalar.activation(z[:, 4, :], z[:, 3, :], ACT.Exp).then_inc(tail_a, 1)
                nc.scalar.activation(keep["a_log"][:], keep["a_log"][:], ACT.Exp).then_inc(tail_a, 1)
                act.wait_ge(tail_a, 2)
                nc.scalar.activation(z[:, 5, :], z[:, 4, :], ACT.Ln, bias=1.0).then_inc(tail_a, 1)

            @block.gpsimd
            def _(pool):
                low.credit(pool)
                with pool.Fori(0, turns) as i:
                    for u in range(2):
                        w = i * 2 + u
                        pool.wait_ge(high.sem, high.at(w, 1))
                        cut = bass.ds(w * P, P)
                        nc.gpsimd.tensor_tensor(hl[:, :, cut], ht[:, u, :, :], hh[:, :, cut].bitcast(F32), ALU.subtract).then_inc(low.sem, 1)

            @block.tensor
            def _(pe):
                for t in (turned, small):
                    t.credit(pe)
                pe.wait_ge(w_in, 16)
                with pe.Fori(0, turns) as i:
                    for u in range(2):
                        w = i * 2 + u
                        pe.wait_ge(scaled.sem, w + 3)
                        pe.wait_ge(weighted.sem, weighted.at(w, -2))
                        for k in range(K):
                            t = nc.tensor.transpose(ps[2 * u + k // 4][:, (k % 4) * P:(k % 4 + 1) * P], xn[:, u, k * P:(k + 1) * P], keep["ident"][:])
                        t.then_inc(turned.sem, 1)
                    for u in range(2):
                        w = i * 2 + u
                        pe.wait_ge(weighted.sem, weighted.at(w, 2))
                        pe.wait_ge(kept.sem, kept.at(w, -1))
                        for k in range(K):
                            t = nc.tensor.matmul(ps[4 + u][:, 0:2 * V], ht[:, u, k, :], wsm[:, k, :], start=(k == 0), stop=(k == K - 1))
                        t.then_inc(small.sem, 1)

            @block.vector
            def _(dve):
                scaled_credit = 2
                dve.sem_inc(scaled.sem, scaled_credit)
                for t in (weighted, kept):
                    t.credit(dve)

                def normalise(w, u):
                    dve.wait_ge(rstd.sem, rstd.at(w, 2))
                    nc.vector.tensor_scalar(xn[:, u, :], xin[:, u, :], stat[:, u, 2:3], None, ALU.mult).then_inc(scaled.sem, 1)

                def weigh(i, u):
                    w = i * 2 + u
                    dve.wait_ge(turned.sem, turned.at(w, 1))
                    dve.wait_ge(h_out[u].sem, i * 16 + 16)
                    dve.wait_ge(low.sem, low.at(w, -1))
                    dve.wait_ge(small.sem, small.at(w, -1))
                    for b in range(2):
                        nc.vector.tensor_tensor(ht[:, u, 4 * b:4 * b + 4, :], ps[2 * u + b][:].rearrange("p (k n) -> p k n", n=P),
                                                spread(nw[:, 4 * b:4 * b + 4], P), ALU.mult).then_inc(weighted.sem, 1)

                def keep_small(w, u):
                    dve.wait_ge(small.sem, small.at(w, 1))
                    nc.vector.tensor_copy(keep["ab"][:, bass.ds(w * (2 * V), 2 * V)], ps[4 + u][:, 0:2 * V]).then_inc(kept.sem, 1)

                for u in range(2):
                    normalise(u, u)
                with dve.Fori(0, turns - 1) as i:
                    for u in range(2):
                        weigh(i, u)
                        normalise(i * 2 + (u + 2), u)
                    for u in range(2):
                        keep_small(i * 2 + u, u)
                for u in range(2):
                    weigh(turns - 1, u)
                for u in range(2):
                    keep_small(dm.win - 2 + u, u)
                dve.wait_ge(kept.sem, kept.at(dm.win, 0))
                ab = keep["ab"][:, 0:dm.win * 2 * V].rearrange("p (w c) -> p w c", c=2 * V)
                zz = lambda k: z[:, k, :].rearrange("p (w c) -> p w c", c=V)
                over = lambda t: free_ap(t[:], 0, [[0, dm.win], [1, V]])
                nc.vector.tensor_copy(zz(0), ab[:, :, 0:V]).then_inc(tail_v, 1)
                nc.vector.tensor_tensor(zz(2), ab[:, :, V:2 * V], over(keep["dt_bias"]), ALU.add).then_inc(tail_v, 1)
                dve.wait_ge(tail_v, 2)
                nc.vector.scalar_tensor_tensor(z[:, 3, :], z[:, 2, :], -1.0, z[:, 2, :], ALU.mult, ALU.min).then_inc(tail_v, 1)
                dve.wait_ge(tail_a, 4)
                dve.wait_ge(tail_v, 3)
                nc.vector.scalar_tensor_tensor(z[:, 2, :], z[:, 2, :], 0.0, z[:, 5, :], ALU.max, ALU.add).then_inc(tail_v, 1)
                nc.vector.tensor_scalar(z[:, 1, :], z[:, 1, :], 1.0, None, ALU.add).then_inc(tail_v, 1)
                nc.vector.tensor_scalar(keep["a_log"][:], keep["a_log"][:], -1.0, None, ALU.mult).then_inc(tail_v, 1)
                dve.wait_ge(tail_v, 6)
                nc.vector.memset(keep["ab"][:, dm.win * 2 * V:], 0.0).then_inc(tail_v, 1)
                nc.vector.reciprocal(z[:, 0, :], z[:, 1, :]).then_inc(tail_v, 1)
                nc.vector.tensor_tensor(ab[:, :, 0:V], zz(2), over(keep["a_log"]), ALU.mult).then_inc(tail_v, 1)
                dve.wait_ge(tail_v, 9)
                nc.vector.tensor_copy(ab[:, :, V:2 * V], zz(0)).then_inc(tail_v, 1)


def branch_tiles(dm):
    at, n = {}, 0
    for name, k in (("hk", dm.hh), ("hq", dm.hh), ("h_neg_g", dm.hh), ("hg", dm.hh), ("hv", dm.hh), ("hz", dm.hh),
                    ("q", dm.qh), ("k", dm.qh), ("v", dm.vh), ("z", dm.vh)):
        at[name] = n
        n += k
    at["end"] = n
    return at


def pass_on(engine, sem, value, *others):
    engine.wait_ge(sem, value)
    for other in others:
        engine.sem_inc(other, 1)


def project(nc, dm, io, keep, hh, hl, s_dram, y_dram):
    rows, tiles, K, T = vector_rows(dm), branch_tiles(dm), dm.kt, dm.blk
    groups = dm.wa
    assert dm.wa == dm.hh == dm.qh and T == 4
    units = [("copy_c", dm.a_c, 1, None), ("x", dm.a_x, 1, None), ("gate_a", dm.a_z, 1, None), ("b", dm.a_b, 1, None),
             ("silu", dm.b_q, 1, tiles["hq"]), ("forget", dm.b_f, 1, None), ("plain", dm.b_i, 1, tiles["hv"]),
             ("silu", dm.b_z, 1, tiles["hz"]), ("conv", dm.c_q, 1, tiles["q"]), ("conv", dm.c_k, 1, tiles["k"]),
             ("conv", dm.c_v, 2, tiles["v"]), ("conv", dm.c_v + P, 2, tiles["v"] + 1),
             ("silu", dm.c_z, 2, tiles["z"]), ("silu", dm.c_z + P, 2, tiles["z"] + 1)]
    U = len(units)
    conv_tile = {8: (0, 1), 9: (dm.qh, 1), 10: (2 * dm.qh, 2), 11: (2 * dm.qh + 1, 2)}
    results = []
    for m, (kind, *_) in enumerate(units):
        for t in range(T):
            results += [(m, t, part) for part in {"copy_c": [], "x": [], "gate_a": [], "forget": ["k", "g", "neg_g"]}.get(kind, ["y"])]
    RING = 4
    assert len(results) % RING == 0
    uses = len(results) // RING
    from_dve = [r for r in results if units[r[0]][0] in ("b", "forget")]

    def per_unit(kinds):
        return [m for m, u in enumerate(units) if u[0] in kinds]

    class Steps:

        def __init__(self, sem, kinds):
            self.sem, self.of = sem, per_unit(kinds)

        def at(self, group, m, t):
            return group * (T * len(self.of)) + (T * self.of.index(m) + t + 1)

    with ExitStack() as c:
        sb = lambda n, s, d=F32: c.enter_context(nc.sbuf_tensor(n, s, d))
        stage = sb("w_stage", [P, 2, K, P])
        wh, wl = sb("w_high", [P, 2, K, P], F32R), sb("w_low", [P, 2, K, P], F32R)
        hist = sb("hist", [P, 2, 3 + dm.seq])
        cb = sb("cb", [P, T, BLK])
        act_z = sb("act_z", [P, 2, BLK])
        ex = sb("ex", [P, 2, BLK])
        tap = sb("tap", [P, 2, BLK])
        fg = sb("fg", [P, 2, BLK])
        ring = sb("ring", [P, RING, BLK])
        fresh = sb("fresh", [P, BLK])
        ps = [c.enter_context(nc.psum_tensor(f"ps_p{i}", [P, BLK], F32)) for i in range(T)]
        sem = lambda n: c.enter_context(nc.semaphore("p_" + n))
        w_in = [sem(f"w_in{s}") for s in range(2)]
        w_high = sem("w_high")
        w_ready, acc = Ahead(sem("w_ready"), 1, 2), Ahead(sem("acc"), T, 2)
        bank_free = [Ahead(sem(f"bank_free{t}"), 1, 1) for t in range(T)]
        copied = Steps(sem("copied"), ("copy_c", "plain", "conv"))
        silued = Steps(sem("silued"), ("gate_a", "silu", "conv"))
        gated = Steps(sem("gated"), ("gate_a",))
        exped = Steps(sem("exped"), ("forget",))
        tapped = Steps(sem("tapped"), ("conv",))
        ranged, logged = Steps(sem("ranged"), ("forget",)), Steps(sem("logged"), ("forget",))
        ready = sem("ready")
        out_done = [sem(f"out_done{r}") for r in range(RING)]
        masks_set, masks_cut = sem("masks_set"), sem("masks_cut")
        zeroed, step, passed, passed_p = sem("zeroed"), sem("step"), sem("passed"), sem("passed_p")

        def slot(m, t, part):
            return results.index((m, t, part)) % RING

        def free_value(g, m, t, part):
            return g * (16 * uses) + (16 * (results.index((m, t, part)) // RING) + 16)

        def ready_value(g, m, t, part):
            return g * len(from_dve) + (from_dve.index((m, t, part)) + 1)

        def unit_no(g, m):
            return g * U + m

        with nc.Block() as block:
            @block.sync
            def _(sp):
                with sp.Fori(0, groups) as g:
                    for m, (_, col, by, _) in enumerate(units):
                        wait_apart(sp, w_ready.sem, w_ready.at(unit_no(g, m), -1), passed)
                        sp.dma_start(stage[:, m % 2, :, :], io["w_in"][0, :, bass.ds(g * (by * P) + col, P)].rearrange("(k p) c -> p k c", p=P)
                                     ).then_inc(w_in[m % 2], 16)

            @block.gpsimd
            def _(pool):
                w_ready.credit(pool)
                pool.memset(hist[:, :, 0:3], 0.0).then_inc(zeroed, 1)
                pool.memset(fresh[:], 1.0).then_inc(zeroed, 1)
                pool.wait_ge(zeroed, 2)
                pool.memset(free_ap(fresh[:], 0, [[P, BLK // P], [1, 1]]), 0.0).then_inc(zeroed, 1)
                with pool.Fori(0, groups * U // 2) as i:
                    for s in range(2):
                        n = i * 2 + s
                        pool.wait_ge(acc.sem, acc.at(n, -T))
                        wait_apart(pool, w_in[s], i * 16 + 16, passed_p)
                        nc.gpsimd.tensor_scalar(wh[:, s, :, :], stage[:, s, :, :], 1.0, None, ALU.mult).then_inc(w_high, 1)
                        pool.wait_ge(w_high, n + 1)
                        nc.gpsimd.tensor_tensor(wl[:, s, :, :], stage[:, s, :, :], wh[:, s, :, :].bitcast(F32), ALU.subtract).then_inc(w_ready.sem, 1)
                fill_masks(pool, keep["masks"], masks_set, masks_cut)

            @block.tensor
            def _(pe):
                acc.credit(pe)
                with pe.Fori(0, groups * U // 2) as i:
                    for s in range(2):
                        n = i * 2 + s
                        pe.wait_ge(w_ready.sem, w_ready.at(n, 1))
                        for t in range(T):
                            pe.wait_ge(bank_free[t].sem, bank_free[t].at(n, 0))
                            cut = slice(t * BLK, (t + 1) * BLK)
                            for k in range(K):
                                for a, (w, h) in enumerate(((wh, hh), (wl, hh), (wh, hl))):
                                    last = nc.tensor.matmul(ps[t][:], w[:, s, k, :], h[:, k, cut], start=(k == 0 and a == 0),
                                                            stop=(k == K - 1 and a == 2))
                            last.then_inc(acc.sem, 1)

            @block.scalar
            def _(act):
                nc.scalar.preload_act_table_set(TABLES)
                for r in range(RING):
                    act.sem_inc(out_done[r], 16)
                act.wait_ge(zeroed, 3)
                with act.Fori(0, groups) as g:
                    def store(m, t, part, tile, by, dram):
                        kind, r = units[m][0], slot(m, t, part)
                        if kind == "plain":
                            act.wait_ge(copied.sem, copied.at(g, m, t))
                        elif kind in ("silu", "conv"):
                            act.wait_ge(silued.sem, silued.at(g, m, t))
                        else:
                            act.wait_ge(ready, ready_value(g, m, t, part))
                        nc.scalar.dma_start(dram[bass.ds(g * by + tile, 1), :, t * BLK:(t + 1) * BLK].rearrange("o p n -> p (o n)"),
                                            ring[:, r, :]).then_inc(out_done[r], 16)

                    nc.scalar.preload_act_table_set(SILU_TABLES)
                    for m, (kind, _, by, tile) in enumerate(units):
                        n = unit_no(g, m)
                        if kind == "forget":
                            nc.scalar.preload_act_table_set(TABLES)
                        for t in range(T + 2):
                            bank, cut = t < T, slice(3 + t * BLK, 3 + (t + 1) * BLK)
                            if bank and kind not in ("x", "b"):
                                act.wait_ge(acc.sem, acc.at(n, t + 1))
                            if kind == "copy_c" and bank:
                                nc.scalar.activation(cb[:, t, :], ps[t][:], ACT.Copy).then_inc(copied.sem, 1)
                                pass_on(act, copied.sem, copied.at(g, m, t), bank_free[t].sem)
                            elif kind == "gate_a" and bank:
                                if t >= 2:
                                    act.wait_ge(gated.sem, gated.at(g, m, t - 2))
                                nc.scalar.activation(act_z[:, t % 2, :], ps[t][:], ACT.Silu).then_inc(silued.sem, 1)
                                pass_on(act, silued.sem, silued.at(g, m, t), bank_free[t].sem)
                            elif kind == "b" and bank:
                                store(m, t, "y", 0, 1, y_dram)
                            elif kind in ("silu", "plain"):
                                if bank:
                                    func, done = (ACT.Silu, silued) if kind == "silu" else (ACT.Copy, copied)
                                    act.wait_ge(out_done[slot(m, t, "y")], free_value(g, m, t, "y"))
                                    nc.scalar.activation(ring[:, slot(m, t, "y"), :], ps[t][:], func).then_inc(done.sem, 1)
                                    pass_on(act, done.sem, done.at(g, m, t), bank_free[t].sem)
                                if 1 <= t <= T:
                                    store(m, t - 1, "y", tile, by, s_dram)
                            elif kind == "forget":
                                if bank:
                                    nc.scalar.activation(ex[:, t % 2, :], ps[t][:], ACT.Exp, scale=-1.0).then_inc(exped.sem, 1)
                                    pass_on(act, exped.sem, exped.at(g, m, t), bank_free[t].sem)
                                    act.wait_ge(ranged.sem, ranged.at(g, m, t))
                                    nc.scalar.activation(fg[:, 0, :], fg[:, 0, :], ACT.Ln)
                                    nc.scalar.activation(fg[:, 1, :], fg[:, 1, :], ACT.Ln, scale=1.0 / F_SPLIT).then_inc(logged.sem, 1)
                                if 1 <= t <= T:
                                    for part, where in (("k", "hk"), ("g", "hg"), ("neg_g", "h_neg_g")):
                                        store(m, t - 1, part, tiles[where], 1, s_dram)
                            elif kind == "conv":
                                if bank:
                                    nc.scalar.activation(hist[:, m % 2, cut], ps[t][:], ACT.Copy).then_inc(copied.sem, 1)
                                    pass_on(act, copied.sem, copied.at(g, m, t), bank_free[t].sem)
                                if 1 <= t <= T:
                                    act.wait_ge(tapped.sem, tapped.at(g, m, t - 1))
                                    act.wait_ge(out_done[slot(m, t - 1, "y")], free_value(g, m, t - 1, "y"))
                                    nc.scalar.activation(ring[:, slot(m, t - 1, "y"), :], tap[:, (t - 1) % 2, :], ACT.Silu).then_inc(silued.sem, 1)
                                if t >= 2:
                                    store(m, t - 2, "y", tile, by, s_dram)
                        if kind == "forget":
                            nc.scalar.preload_act_table_set(SILU_TABLES)
                for r in range(RING):
                    act.wait_ge(out_done[r], 16 * uses * groups + 16)

            @block.vector
            def _(dve):
                for t in range(T):
                    bank_free[t].credit(dve)
                dve.wait_ge(zeroed, 3)
                links = 84
                with dve.Fori(0, groups) as g:
                    chain = [0]

                    def link(ins):
                        chain[0] += 1
                        ins.then_inc(step, 1)
                        dve.wait_ge(step, g * links + chain[0])

                    col = lambda name, i, at, by: keep["cols"][:, bass.ds(g * by + (rows[name] + i + at), 1)]
                    for m, (kind, _, by, tile) in enumerate(units):
                        n = unit_no(g, m)

                        def result(t, part="y"):
                            r = slot(m, t, part)
                            dve.wait_ge(out_done[r], free_value(g, m, t, part))
                            return ring[:, r, :]

                        def conv(out, h, t, taps, name, at, by):
                            per_tap = keep_tiles[name]
                            for i in range(taps):
                                src = hist[:, h, 3 + t * BLK - (taps - 1 - i):3 + (t + 1) * BLK - (taps - 1 - i)]
                                w = col(name, i * per_tap, at, by)
                                if i == 0:
                                    link(nc.vector.tensor_scalar(out, src, w, None, ALU.mult))
                                elif i < taps - 1:
                                    link(nc.vector.scalar_tensor_tensor(out, src, w, out, ALU.mult, ALU.add))
                                else:
                                    return nc.vector.scalar_tensor_tensor(out, src, w, out, ALU.mult, ALU.add)

                        keep_tiles = {"conv_a": dm.wa, "conv_c": 2 * dm.qh + dm.vh}
                        if kind == "x":
                            for t in range(T):
                                dve.wait_ge(copied.sem, copied.at(g, 0, t))
                                dve.wait_ge(acc.sem, acc.at(n, t + 1))
                                link(nc.vector.tensor_tensor(hist[:, 1, 3 + t * BLK:3 + (t + 1) * BLK], cb[:, t, :], ps[t][:], ALU.mult))
                                dve.sem_inc(bank_free[t].sem, 1)
                                link(conv(cb[:, t, :], 1, t, 3, "conv_a", 0, 1))
                        elif kind == "gate_a":
                            for t in range(T):
                                dve.wait_ge(silued.sem, silued.at(g, m, t))
                                nc.vector.tensor_tensor(cb[:, t, :], cb[:, t, :], act_z[:, t % 2, :], ALU.mult).then_inc(gated.sem, 1)
                        elif kind == "b":
                            for t in range(T):
                                if t == 0:
                                    dve.wait_ge(gated.sem, gated.at(g, m - 1, T - 1))
                                dve.wait_ge(acc.sem, acc.at(n, t + 1))
                                nc.vector.tensor_tensor(result(t), ps[t][:], cb[:, t, :], ALU.mult).then_inc(ready, 1)
                                pass_on(dve, ready, ready_value(g, m, t, "y"), bank_free[t].sem)
                        elif kind == "forget":
                            for t in range(T):
                                e = ex[:, t % 2, :]
                                dve.wait_ge(exped.sem, exped.at(g, m, t))
                                link(nc.vector.tensor_scalar(e, e, 1.0, None, ALU.add))
                                link(nc.vector.reciprocal(e, e))
                                link(nc.vector.tensor_scalar(e, e, keep["one_less_lb"][:, bass.ds(g, 1)], keep["lb"][:, bass.ds(g, 1)], ALU.mult, ALU.add))
                                nc.vector.tensor_scalar(result(t, "k"), e, -1.0, 1.0, ALU.mult, ALU.add).then_inc(ready, 1)
                                link(nc.vector.tensor_scalar(fg[:, 1, :], e, MIN_F, F_SPLIT, ALU.max, ALU.min))
                                nc.vector.tensor_scalar(fg[:, 0, :], e, F_SPLIT, None, ALU.max).then_inc(ranged.sem, 1)
                                dve.wait_ge(logged.sem, logged.at(g, m, t))
                                link(nc.vector.tensor_tensor(fg[:, 0, :], fg[:, 0, :], fg[:, 1, :], ALU.add))
                                out = result(t, "g")
                                nc.vector.tensor_tensor_scan(out, fresh[:], fg[:, 0, :], 0.0, ALU.mult, ALU.add).then_inc(ready, 1)
                                dve.wait_ge(ready, ready_value(g, m, t, "g"))
                                nc.vector.tensor_scalar(result(t, "neg_g"), out, -1.0, None, ALU.mult).then_inc(ready, 1)
                        elif kind == "conv":
                            at, by_c = conv_tile[m]
                            for t in range(T):
                                dve.wait_ge(copied.sem, copied.at(g, m, t))
                                if t >= 2:
                                    dve.wait_ge(silued.sem, silued.at(g, m, t - 2))
                                conv(tap[:, t % 2, :], m % 2, t, 4, "conv_c", at, by_c).then_inc(tapped.sem, 1)
                    assert chain[0] == links, chain[0]
def recur(nc, dm, keep, s_dram, y_dram):
    tiles, H, Q, V = branch_tiles(dm), dm.hh, dm.qh, dm.vh
    assert H == 4 and Q == 4 and V == 8
    NH, NC = 6 * H, 2 * Q + 2 * V
    KH, QH, NG, GG, VH, ZH = (tiles[k] for k in ("hk", "hq", "h_neg_g", "hg", "hv", "hz"))
    QC, VC, ZC = 0, 2 * Q, 2 * Q + V
    HOP = H * P
    last = P - 1
    hw = keep["head_w"]
    with ExitStack() as c:
        sb = lambda n, s, d=F32: c.enter_context(nc.sbuf_tensor(n, s, d))
        more_masks = {"pair": sb("pair", [P, 2, P]), "upper": sb("upper", [P, LEVELS, P]), "lower": sb("lower", [P, LEVELS - 1, P])}
        masks = {**keep["masks"], **more_masks}
        masks_set, masks_cut = (c.enter_context(nc.semaphore("r_" + n)) for n in ("masks_set", "masks_cut"))
        hin, cin = sb("hin", [P, 2, NH, P]), sb("cin", [P, 2, NC, P])
        lbw = sb("lbw", [P, 2 * V])
        la_parts = sb("la_parts", [P, 2, V], F32R)
        la_t = sb("la_t", [P, 2, V, P], F32R)
        ones_r, later_r = sb("ones_r", [P, P], F32R), sb("later_r", [P, P], F32R)
        dec, eg = sb("dec", [P, V, P]), sb("eg", [P, V, P])
        ecol = sb("ecol", [P, 2 * V])
        neg_eg, bk = sb("neg_eg", [P, V]), sb("bk", [P, V])
        sq, rn, qkn = sb("sq", [P, 2, Q * P]), sb("rn", [P, 2, Q * P]), sb("qkn", [P, 2, Q * P])
        kqm = sb("kqm", [P, Q, 2 * P])
        an = sb("an", [P, V, 2, P])
        R, TT, W = sb("R", [P, V, P]), sb("T", [P, V, P]), sb("W", [P, V, P])
        vt, kt = sb("vt", [P, V, P]), sb("kt", [P, Q, P])
        qg, ks, r, e = sb("qg", [P, V, P]), sb("ks", [P, V, P]), sb("r", [P, V, P]), sb("e", [P, V, P])
        S, sqc, rnc, t1c = sb("S", [P, V, P]), sb("sqc", [P, V, P]), sb("rnc", [P, V, P]), sb("t1c", [P, V, P])
        yc, yh = sb("yc", [P, 2, V, P]), sb("yh", [P, 2, H, P])
        dx, hx, kql = sb("dx", [P, 2, HOP]), sb("hx", [P, 2, HOP]), sb("kql", [P, 2, HOP])
        egh, qe, ke, A = sb("egh", [P, H, P]), sb("qe", [P, HOP]), sb("ke", [P, H, P]), sb("A", [P, H, P])
        vht, kht, sqh, rnh, t1h, SH = (sb(n, [P, H, P]) for n in ("vht", "kht", "sqh", "rnh", "t1h", "SH"))
        bank = lambda n: c.enter_context(nc.psum_tensor("b_" + n, [P, 4, P], F32))
        G, HB, M = [bank(f"g{i}") for i in range(2)], [bank(f"h{i}") for i in range(2)], [bank(f"m{i}") for i in range(4)]

        sems = {}

        def count(engine, **per):
            for n, k in per.items():
                sems[n] = (Ahead(c.enter_context(nc.semaphore("r_" + n)), k), engine)

        count("pe", m_col=1, m_g=4, m_ssq=2, m_vt=2, m_kq=2, m_kt=1, m_t=2, m_w=12, m_z=12, m_r=10, m_hs=8, m_ks=2,
              m_hvt=1, m_hkt=1, m_ho=1, m_hds=1, m_e=2, m_o=2, m_ds=2, m_hn=1, m_n=2)
        count("act", e_col=1, e_g=4, rn_ready=4, e_h=1, vt_ready=2, kt_ready=1, t_ready=2, w_ready=12, r_ready=10,
              h_exp=8, h_turned=2, e_ready=2, sqh_ready=1, sqc_ready=2, rnh_ready=2, rnc_ready=4)
        count("pool", sq_ready=1, r_init=1, dx_ready=8, qe_ready=1, ke_ready=1, qg_ready=1, ks_ready=1)
        count("dve", lb=1, la_split=2, la_ready=2, qkn_ready=2, cols_ready=2, kqm_ready=2, an_ready=8, r_pair=2, h_kq=7, h_pred=8,
              t_pred=10, r_done=2, res=8, hs_done=4, t1h_ready=1, y_h=1, s_done=8, t1c_ready=2, y_c=2)
        h_in = [c.enter_context(nc.semaphore(f"r_h_in{u}")) for u in range(2)]
        c_in = [c.enter_context(nc.semaphore(f"r_c_in{u}")) for u in range(2)]
        yh_out = [c.enter_context(nc.semaphore(f"r_yh_out{u}")) for u in range(2)]
        yc_out = [c.enter_context(nc.semaphore(f"r_yc_out{u}")) for u in range(2)]
        s_zero, passed, passed_sp = (c.enter_context(nc.semaphore("r_" + n)) for n in ("s_zero", "passed", "passed_sp"))

        def wait(engine, w, name, k):
            engine.wait_ge(sems[name][0].sem, sems[name][0].at(w, k))

        def sem(name):
            return sems[name][0].sem

        def credits(engine, name):
            for t, of in sems.values():
                if of == name:
                    t.credit(engine)

        flat = lambda t: t[:].rearrange("p a b -> p (a b)")
        four = lambda t, g: t[:, 4 * g:4 * g + 4, :]

        def level_ap(tile, u, at, off, hop, inner):
            return free_ap(tile[:, u, at, :], off, [hop[0], hop[1], inner])

        turns = dm.win // 2
        ds = dm.win
        with nc.Block() as block:
            @block.sync
            def _(sp):
                for u in range(2):
                    sp.sem_inc(yh_out[u], 16)
                    sp.sem_inc(yc_out[u], 16)
                n_h = 6 * H

                def load(w, u):
                    cut = bass.ds(w * P, P)
                    sp.dma_start(hin[:, u, :, :], s_dram[0:n_h, :, cut].rearrange("t p n -> p t n")).then_inc(h_in[u], 16)
                    sp.dma_start(cin[:, u, :, :], s_dram[n_h:n_h + NC, :, cut].rearrange("t p n -> p t n")).then_inc(c_in[u], 16)

                def store(w, u):
                    cut = bass.ds(w * P, P)
                    wait_apart(sp, sem("y_h"), sems["y_h"][0].at(w, 1), passed_sp)
                    sp.dma_start(y_dram[dm.wa:dm.wa + H, :, cut].rearrange("t p n -> p t n"), yh[:, u, :, :]).then_inc(yh_out[u], 16)
                    wait_apart(sp, sem("y_c"), sems["y_c"][0].at(w, 2), passed_sp)
                    sp.dma_start(y_dram[dm.wa + H:dm.wa + H + V, :, cut].rearrange("t p n -> p t n"), yc[:, u, :, :]).then_inc(yc_out[u], 16)

                for u in range(2):
                    load(u, u)
                with sp.Fori(0, turns - 1) as i:
                    for u in range(2):
                        store(i * 2 + u, u)
                        load(i * 2 + (u + 2), u)
                for u in range(2):
                    store(dm.win - 2 + u, u)
                for u in range(2):
                    sp.wait_ge(yh_out[u], 16 * turns + 16)
                    sp.wait_ge(yc_out[u], 16 * turns + 16)

            @block.gpsimd
            def _(pool):
                credits(pool, "pool")
                fill_masks(pool, more_masks, masks_set, masks_cut)
                tt = nc.gpsimd.tensor_tensor
                with pool.Fori(0, turns) as i:
                    for u in range(2):
                        w = i * 2 + u
                        pool.wait_ge(h_in[u], i * 16 + 16)
                        pool.wait_ge(c_in[u], i * 16 + 16)
                        wait(pool, w, "m_ssq", 0)
                        qk = cin[:, u, QC:QC + 2 * Q, :]
                        tt(sq[:].rearrange("p a (b n) -> p (a b) n", n=P), qk, qk, ALU.mult).then_inc(sem("sq_ready"), 1)
                        for l in range(LEVELS):
                            b = 1 << l
                            wait(pool, w, "h_exp", l - 1)
                            left = free_ap(hin[:, u, NG, :], 0, [[2 * b, HOP // (2 * b)], [HOP + b, 2], [1, b]])
                            mid = free_ap(hin[:, u, NG, :], b - 1, [[2 * b, HOP // (2 * b)], [HOP, 2], [0, b]])
                            out = dx[:, l % 2, :].rearrange("p (n a b) -> p n a b", a=2, b=b)
                            tt(out, left, mid, ALU.subtract).then_inc(sem("dx_ready"), 1)
                            if l == 0:
                                wait(pool, w, "m_e", 0)
                                tt(R[:], free_ap(keep["ident"][:], 0, [[0, V], [1, P]]), free_ap(keep["ident"][:], 0, [[0, V], [1, P]]),
                                   ALU.mult).then_inc(sem("r_init"), 1)
                        wait(pool, w, "h_exp", LEVELS - 1)
                        end = free_ap(hin[:, u, NG, :], last, [[P, H], [0, P]])
                        tt(dx[:, LEVELS % 2, :].rearrange("p (h n) -> p h n", n=P), hin[:, u, NG:NG + H, :], end, ALU.subtract).then_inc(sem("dx_ready"), 1)
                        wait(pool, w, "e_h", 1)
                        wait(pool, w, "m_ho", 0)
                        tt(qe[:].rearrange("p (h n) -> p h n", n=P), hin[:, u, QH:QH + H, :], egh[:], ALU.mult).then_inc(sem("qe_ready"), 1)
                        wait(pool, w, "qkn_ready", 2)
                        wait(pool, w, "e_g", 4)
                        wait(pool, w, "m_o", 0)
                        tt(qg[:].rearrange("p (a b) n -> p a b n", b=2), free_ap(qkn[:, 0, :], 0, [[P, Q], [0, 2], [1, P]]),
                           eg[:].rearrange("p (a b) n -> p a b n", b=2), ALU.mult).then_inc(sem("qg_ready"), 1)
                        wait(pool, w, "kt_ready", 1)
                        wait(pool, w, "cols_ready", 2)
                        wait(pool, w, "m_ds", 0)
                        tt(ks[:].rearrange("p (a b) n -> p a b n", b=2), free_ap(kt[:], 0, [[P, Q], [0, 2], [1, P]]),
                           free_ap(bk[:], 0, [[2, Q], [1, 2], [0, P]]), ALU.mult).then_inc(sem("ks_ready"), 1)
                        wait(pool, w, "h_exp", LEVELS + 1)
                        wait(pool, w, "m_hkt", 0)
                        tt(flat(ke), hin[:, u, KH:KH + H, :].rearrange("p h n -> p (h n)"), hx[:, LEVELS % 2, :], ALU.mult).then_inc(sem("ke_ready"), 1)

            @block.tensor
            def _(pe):
                credits(pe, "pe")
                mm, turn, ident = nc.tensor.matmul, nc.tensor.transpose, keep["ident"][:]

                def sum_parts(bank, which, g):
                    for part in range(2):
                        x = mm(bank[:], which[:], four(la_t[:, part, :, :], g), start=(part == 0), stop=(part == 1))
                    return x

                pe.wait_ge(s_zero, 4)
                with pe.Fori(0, turns) as i:
                    for u in range(2):
                        w = i * 2 + u
                        def scores(l):
                            if l == 0:
                                pe.wait_ge(h_in[u], i * 16 + 16)
                                wait(pe, w, "t1h_ready", 0)
                            else:
                                wait(pe, w, "h_kq", l)
                                if l == 1:
                                    wait(pe, w, "rnh_ready", 0)
                                else:
                                    wait(pe, w, "h_pred", l - 1)
                            for h in range(H):
                                if l == 0:
                                    a, b = hin[:, u, KH + h, :], hin[:, u, QH + h, :]
                                else:
                                    a = b = kql[:, l % 2, h * P:(h + 1) * P]
                                x = mm(HB[l % 2][:, h, :], a, b, start=True, stop=True)
                            x.then_inc(sem("m_hs"), 1)

                        wait(pe, w, "sq_ready", 1)
                        wait(pe, w, "s_done", 0)
                        for g in range(2):
                            mm(M[g][:], keep["ones"][:], sq[:, g, :], start=True, stop=True).then_inc(sem("m_ssq"), 1)
                        wait(pe, w, "la_ready", 2)
                        wait(pe, w, "t1c_ready", 0)
                        for g in range(2):
                            sum_parts(M[2 + g], ones_r, g).then_inc(sem("m_g"), 1)
                        for g in range(2):
                            wait(pe, w, "rn_ready", 2 * g + 1)
                            sum_parts(M[g], later_r, g).then_inc(sem("m_g"), 1)
                        scores(0)
                        wait(pe, w, "rnc_ready", 0)
                        mm(G[0][:, 0, 0:V], masks["causal"][:], lbw[:, 0:V], start=True, stop=True)
                        mm(G[0][:, 0, V:2 * V], masks["later"][:], lbw[:, 0:V], start=True, stop=True).then_inc(sem("m_col"), 1)
                        pe.wait_ge(c_in[u], i * 16 + 16)
                        for g in range(2):
                            wait(pe, w, "e_g", g + 1)
                            for h in range(4):
                                x = turn(M[2 + g][:, h, :], cin[:, u, VC + 4 * g + h, :], ident)
                            x.then_inc(sem("m_vt"), 1)
                        wait(pe, w, "qkn_ready", 2)
                        for g in range(2):
                            wait(pe, w, "e_g", 3 + g)
                            for j in range(2):
                                q = 2 * g + j
                                x = mm(M[g][:, 2 * j:2 * j + 2, :], qkn[:, 1, q * P:(q + 1) * P],
                                       free_ap(qkn[:, 0, :], q * P, [[Q * P, 2], [1, P]]), start=True, stop=True)
                            x.then_inc(sem("m_kq"), 1)
                        for q in range(Q):
                            x = turn(G[1][:, q, :], qkn[:, 1, q * P:(q + 1) * P], ident)
                        x.then_inc(sem("m_kt"), 1)
                        def product_ks(g):
                            wait(pe, w, "kqm_ready", g + 1)
                            for j in range(2):
                                q = 2 * g + j
                                x = mm(M[g][:, 2 * j:2 * j + 2, :], qkn[:, 1, q * P:(q + 1) * P], S[:, 2 * q:2 * q + 2, :], start=True, stop=True)
                            x.then_inc(sem("m_ks"), 1)

                        scores(1)
                        product_ks(0)
                        product_ks(1)
                        for g in range(2):
                            if g == 0:
                                wait(pe, w, "e_col", 1)
                            else:
                                wait(pe, w, "kt_ready", 1)
                            wait(pe, w, "r_pair", g + 1)
                            for h in range(4):
                                x = turn(G[g][:, h, :], R[:, 4 * g + h, :], ident)
                            x.then_inc(sem("m_t"), 1)
                        def turn_hv():
                            wait(pe, w, "vt_ready", 2)
                            for h in range(H):
                                x = turn(M[2][:, h, :], hin[:, u, VH + h, :], ident)
                            x.then_inc(sem("m_hvt"), 1)

                        for l in range(1, LEVELS):
                            fin = l == LEVELS - 1
                            for g in range(2):
                                if l == 1:
                                    wait(pe, w, "t_ready", g + 1)
                                else:
                                    wait(pe, w, "t_pred", 2 * (l - 2) + g + 1)
                                    wait(pe, w, "r_ready", 2 * (l - 2) + g + 1)
                                for h in range(4 * g, 4 * g + 4):
                                    x = mm(G[g][:, h % 4, :], an[:, h, 1, :], TT[:, h, :], start=True, stop=True)
                                x.then_inc(sem("m_w"), 1)
                            if l == 1:
                                scores(2)
                            for g in range(2):
                                wait(pe, w, "w_ready", 2 * (l - 1) + g + 1)
                                for h in range(4 * g, 4 * g + 4):
                                    if fin:
                                        x = mm(G[g][:, h % 4, :], W[:, h, :], R[:, h, :], start=True, stop=True)
                                    else:
                                        x = mm(G[g][:, h % 4, :], R[:, h, :], W[:, h, :], start=True, stop=True)
                                x.then_inc(sem("m_z"), 1)
                            if not fin:
                                scores(2 + l)
                                for g in range(2):
                                    wait(pe, w, "t_pred", 2 * (l - 1) + g + 1)
                                    for h in range(4 * g, 4 * g + 4):
                                        x = turn(G[g][:, h % 4, :], TT[:, h, :], ident)
                                    x.then_inc(sem("m_r"), 1)
                            if l == 3:
                                turn_hv()
                        wait(pe, w, "ke_ready", 1)
                        for h in range(H):
                            x = turn(M[3][:, h, :], ke[:, h, :], ident)
                        x.then_inc(sem("m_hkt"), 1)
                        wait(pe, w, "qe_ready", 1)
                        wait(pe, w, "h_turned", 2)
                        wait(pe, w, "h_pred", 8)
                        for h in range(H):
                            mm(HB[0][:, h, :], SH[:, h, :], qe[:, h * P:(h + 1) * P], start=True, stop=False)
                            x = mm(HB[0][:, h, :], vht[:, h, :], A[:, h, :], start=False, stop=True)
                        x.then_inc(sem("m_ho"), 1)
                        for h in range(H):
                            x = mm(HB[1][:, h, :], kht[:, h, :], vht[:, h, :], start=True, stop=True)
                        x.then_inc(sem("m_hds"), 1)
                        for g in range(2):
                            wait(pe, w, "r_done", g + 1)
                            wait(pe, w, "res", 4 * g + 4)
                            for h in range(4 * g, 4 * g + 4):
                                x = mm(G[g][:, h % 4, :], R[:, h, :], r[:, h, :], start=True, stop=True)
                            x.then_inc(sem("m_e"), 1)
                        wait(pe, w, "qg_ready", 1)
                        for g in range(2):
                            wait(pe, w, "e_ready", g + 1)
                            for h in range(4 * g, 4 * g + 4):
                                mm(M[2 + g][:, h % 4, :], S[:, h, :], qg[:, h, :], start=True, stop=False)
                                x = mm(M[2 + g][:, h % 4, :], e[:, h, :], an[:, h, 0, :], start=False, stop=True)
                            x.then_inc(sem("m_o"), 1)
                        wait(pe, w, "ks_ready", 1)
                        for g in range(2):
                            for h in range(4 * g, 4 * g + 4):
                                x = mm(M[g][:, h % 4, :], ks[:, h, :], e[:, h, :], start=True, stop=True)
                            x.then_inc(sem("m_ds"), 1)
                        wait(pe, w, "hs_done", 4)
                        wait(pe, w, "sqh_ready", 1)
                        mm(HB[1][:], keep["ones"][:], sqh[:], start=True, stop=True).then_inc(sem("m_hn"), 1)
                        for g in range(2):
                            wait(pe, w, "sqc_ready", g + 1)
                            mm(G[g][:], keep["ones"][:], four(sqc, g), start=True, stop=True).then_inc(sem("m_n"), 1)

            @block.scalar
            def _(act):
                nc.scalar.preload_act_table_set(TABLES)
                credits(act, "act")
                fn, eps = nc.scalar.activation, keep["eps"][:, 0:1]
                with act.Fori(0, turns) as i:
                    for u in range(2):
                        w = i * 2 + u
                        wait(act, w, "qkn_ready", 0)
                        for g in range(2):
                            wait(act, w, "m_ssq", g + 1)
                            fn(rn[:, g, :], flat(M[g]), ACT.Ln, bias=eps).then_inc(sem("rn_ready"), 1)
                            wait(act, w, "rn_ready", 2 * g + 1)
                            fn(rn[:, g, :], rn[:, g, :], ACT.Exp, scale=NEG_HALF).then_inc(sem("rn_ready"), 1)
                        wait(act, w, "s_done", 0)
                        wait(act, w, "hs_done", 0)
                        wait(act, w, "qg_ready", 0)
                        wait(act, w, "ks_ready", 0)
                        for g in range(4):
                            wait(act, w, "m_g", g + 1)
                            fn(four((eg, dec)[g // 2], g % 2), M[(g + 2) % 4][:], ACT.Exp).then_inc(sem("e_g"), 1)
                        wait(act, w, "m_col", 1)
                        fn(ecol[:], G[0][:, 0, 0:2 * V], ACT.Exp).then_inc(sem("e_col"), 1)
                        act.wait_ge(h_in[u], i * 16 + 16)
                        fn(egh[:], hin[:, u, GG:GG + H, :], ACT.Exp).then_inc(sem("e_h"), 1)

                        def level_exp(l):
                            wait(act, w, "dx_ready", l + 1)
                            if l >= 2:
                                wait(act, w, "h_kq", l - 1)
                            fn(hx[:, l % 2, :], dx[:, l % 2, :], ACT.Exp).then_inc(sem("h_exp"), 1)

                        wait(act, w, "ke_ready", 0)
                        level_exp(0)
                        level_exp(1)
                        for g in range(2):
                            wait(act, w, "m_vt", g + 1)
                            fn(four(vt, g), M[2 + g][:], ACT.Copy).then_inc(sem("vt_ready"), 1)
                        wait(act, w, "m_kt", 1)
                        fn(kt[:], G[1][:], ACT.Copy).then_inc(sem("kt_ready"), 1)
                        for g in range(2):
                            wait(act, w, "m_t", g + 1)
                            fn(four(TT, g), G[g][:], ACT.Copy).then_inc(sem("t_ready"), 1)
                        for l in range(1, LEVELS):
                            for g in range(2):
                                wait(act, w, "m_w", 2 * (l - 1) + g + 1)
                                fn(four(W, g), G[g][:], ACT.Copy).then_inc(sem("w_ready"), 1)
                            level_exp(l + 1)
                            if l < LEVELS - 1:
                                for g in range(2):
                                    wait(act, w, "m_r", 2 * (l - 1) + g + 1)
                                    fn(four(R, g), G[g][:], ACT.Copy).then_inc(sem("r_ready"), 1)
                            if l == 3:
                                wait(act, w, "m_hvt", 1)
                                fn(vht[:], M[2][:], ACT.Copy).then_inc(sem("h_turned"), 1)
                        wait(act, w, "m_hkt", 1)
                        fn(kht[:], M[3][:], ACT.Copy).then_inc(sem("h_turned"), 1)
                        wait(act, w, "m_ho", 1)
                        fn(sqh[:], HB[0][:], ACT.Square).then_inc(sem("sqh_ready"), 1)
                        for g in range(2):
                            wait(act, w, "m_e", g + 1)
                            fn(four(e, g), G[g][:], ACT.Copy).then_inc(sem("e_ready"), 1)
                        for g in range(2):
                            wait(act, w, "m_o", g + 1)
                            fn(four(sqc, g), M[2 + g][:], ACT.Square).then_inc(sem("sqc_ready"), 1)
                        mean = 1.0 / P / P
                        wait(act, w, "y_c", 0)
                        wait(act, w, "m_hn", 1)
                        fn(rnh[:], HB[1][:], ACT.Ln, scale=mean, bias=eps).then_inc(sem("rnh_ready"), 1)
                        wait(act, w, "rnh_ready", 1)
                        fn(rnh[:], rnh[:], ACT.Exp, scale=NEG_HALF).then_inc(sem("rnh_ready"), 1)
                        for g in range(2):
                            wait(act, w, "m_n", g + 1)
                            fn(four(rnc, g), G[g][:], ACT.Ln, scale=mean, bias=eps).then_inc(sem("rnc_ready"), 1)
                            wait(act, w, "rnc_ready", 2 * g + 1)
                            fn(four(rnc, g), four(rnc, g), ACT.Exp, scale=NEG_HALF).then_inc(sem("rnc_ready"), 1)

            @block.vector
            def _(dve):
                credits(dve, "dve")
                tt, ts, stt, pred = nc.vector.tensor_tensor, nc.vector.tensor_scalar, nc.vector.scalar_tensor_tensor, nc.vector.copy_predicated
                nc.vector.memset(S[:], 0.0).then_inc(s_zero, 1)
                ts(ones_r[:], keep["ones"][:], 1.0, None, ALU.mult).then_inc(s_zero, 1)
                ts(later_r[:], masks["later"][:], 1.0, None, ALU.mult).then_inc(s_zero, 1)
                nc.vector.memset(SH[:], 0.0).then_inc(s_zero, 1)

                def over(mask, l, n):
                    return free_ap(mask[:, l, :], 0, [[0, n], [1, P]]).bitcast(I32)

                def log_a(w):
                    wait(dve, w, "an_ready", 0)
                    wait(dve, w, "cols_ready", 0)
                    wait(dve, w, "m_col", 0)
                    wait(dve, w, "m_g", 0)
                    wait(dve, w, "la_ready", 0)
                    nc.vector.tensor_copy(lbw[:], keep["ab"][:, bass.ds(w * 2 * V, 2 * V)]).then_inc(sem("lb"), 1)
                    wait(dve, w, "lb", 1)
                    ts(la_parts[:, 0, :], lbw[:, 0:V], 1.0, None, ALU.mult).then_inc(sem("la_split"), 1)
                    wait(dve, w, "la_split", 1)
                    tt(la_parts[:, 1, :], lbw[:, 0:V], la_parts[:, 0, :].bitcast(F32), ALU.subtract).then_inc(sem("la_split"), 1)
                    wait(dve, w, "la_split", 2)
                    for part in range(2):
                        tt(la_t[:, part, :, :], free_ap(masks["causal"][:], 0, [[0, V], [1, P]]), spread(la_parts[:, part, :].bitcast(F32), P),
                           ALU.mult).then_inc(sem("la_ready"), 1)

                log_a(0)
                dve.wait_ge(masks_cut, 2 + 2 * LEVELS + 2 * (LEVELS - 1))
                with dve.Fori(0, turns) as i:
                    for u in range(2):
                        w = i * 2 + u
                        dve.wait_ge(c_in[u], i * 16 + 16)
                        for g in range(2):
                            wait(dve, w, "rn_ready", 2 * g + 2)
                            tt(qkn[:, g, :].rearrange("p (h n) -> p h n", n=P), cin[:, u, QC + Q * g:QC + Q * g + Q, :],
                               rn[:, g, :].rearrange("p (h n) -> p h n", n=P), ALU.mult).then_inc(sem("qkn_ready"), 1)
                        wait(dve, w, "m_ho", 0)
                        wait(dve, w, "m_hs", 1)
                        tt(A[:], HB[0][:], free_ap(keep["ident"][:], 0, [[0, H], [1, P]]), ALU.mult).then_inc(sem("h_pred"), 1)

                        def level_kq(l):
                            b = 1 << l
                            wait(dve, w, "h_exp", l + 1)
                            wait(dve, w, "m_hs", l)
                            kq = free_ap(hin[:, u, KH, :], 0, [[2 * b, HOP // (2 * b)], [HOP + b, 2], [1, b]])
                            shape = lambda t: t[:, (l + 1) % 2, :].rearrange("p (n a b) -> p n a b", a=2, b=b)
                            tt(shape(kql), kq, hx[:, l % 2, :].rearrange("p (n a b) -> p n a b", a=2, b=b), ALU.mult).then_inc(sem("h_kq"), 1)

                        def level_pred(l):
                            wait(dve, w, "h_pred", l + 1)
                            wait_apart(dve, sem("m_hs"), sems["m_hs"][0].at(w, l + 2), passed)
                            pred(A[:], over(masks["upper"], l, H), HB[(l + 1) % 2][:]).then_inc(sem("h_pred"), 1)

                        level_kq(0)
                        for g in range(2):
                            wait(dve, w, "m_kq", g + 1)
                            tt(kqm[:, 2 * g:2 * g + 2, :], M[g][:].rearrange("p (a b) n -> p a (b n)", b=2),
                               free_ap(masks["pair"][:], 0, [[0, 2], [1, 2 * P]]), ALU.mult).then_inc(sem("kqm_ready"), 1)
                        wait(dve, w, "e_g", 4)
                        wait(dve, w, "r_init", 1)
                        for h in range(V):
                            if h % 4 == 0:
                                wait(dve, w, "kqm_ready", h // 4 + 1)
                            stt(an[:, h, :, :], kqm[:, h // 2, :].rearrange("p (a n) -> p a n", a=2), lbw[:, V + h:V + h + 1],
                                free_ap(dec[:, h, :], 0, [[0, 2], [1, P]]), ALU.mult, ALU.mult).then_inc(sem("an_ready"), 1)
                            if h % 4 == 3:
                                wait_apart(dve, sem("an_ready"), sems["an_ready"][0].at(w, h + 1), passed)
                                pred(four(R, h // 4), over(masks["upper"], 0, 4), an[:, h - 3:h + 1, 1, :]).then_inc(sem("r_pair"), 1)
                        level_kq(1)
                        level_pred(0)
                        wait(dve, w, "e_col", 1)
                        ts(neg_eg[:], ecol[:, 0:V], -1.0, None, ALU.mult).then_inc(sem("cols_ready"), 1)
                        tt(bk[:], ecol[:, V:2 * V], lbw[:, V:2 * V], ALU.mult).then_inc(sem("cols_ready"), 1)
                        for l in range(1, LEVELS):
                            fin = l == LEVELS - 1
                            if not fin:
                                level_kq(l + 1)
                            for g in range(2):
                                wait_apart(dve, sem("m_z"), sems["m_z"][0].at(w, 2 * (l - 1) + g + 1), passed)
                                if fin:
                                    pred(four(R, g), over(masks["upper"], l, 4), G[g][:]).then_inc(sem("r_done"), 1)
                                else:
                                    pred(four(TT, g), over(masks["lower"], l, 4), G[g][:]).then_inc(sem("t_pred"), 1)
                            if not fin:
                                level_pred(l)
                            if l == 3:
                                log_a(w + 1)
                        level_pred(LEVELS - 1)
                        wait(dve, w, "vt_ready", 2)
                        for h in range(V):
                            if h % 4 == 0:
                                wait(dve, w, "m_ks", h // 4 + 1)
                            stt(r[:, h, :], M[h // 4][:, h % 4, :], neg_eg[:, h:h + 1], vt[:, h, :], ALU.mult, ALU.add).then_inc(sem("res"), 1)
                        wait(dve, w, "m_hds", 1)
                        for h in range(H):
                            stt(SH[:, h, :], SH[:, h, :], egh[:, h, last:P], HB[1][:, h, :], ALU.mult, ALU.add).then_inc(sem("hs_done"), 1)
                        for h in range(V):
                            if h % 4 == 0:
                                wait(dve, w, "m_ds", h // 4 + 1)
                            stt(S[:, h, :], S[:, h, :], eg[:, h, last:P], M[h // 4][:, h % 4, :], ALU.mult, ALU.add).then_inc(sem("s_done"), 1)
                        wait(dve, w, "y_c", 0)
                        stt(t1h[:], HB[0][:], hw[:, 0:1], hin[:, u, ZH:ZH + H, :], ALU.mult, ALU.mult).then_inc(sem("t1h_ready"), 1)
                        for g in range(2):
                            wait(dve, w, "sqc_ready", g + 1)
                            stt(four(t1c, g), M[2 + g][:], hw[:, 1:2], cin[:, u, ZC + 4 * g:ZC + 4 * g + 4, :], ALU.mult, ALU.mult).then_inc(sem("t1c_ready"), 1)
                        dve.wait_ge(yh_out[u], i * 16 + 16)
                        dve.wait_ge(yc_out[u], i * 16 + 16)
                        wait(dve, w, "rnh_ready", 2)
                        wait(dve, w, "t1h_ready", 1)
                        tt(yh[:, u, :, :], t1h[:], rnh[:], ALU.mult).then_inc(sem("y_h"), 1)
                        for g in range(2):
                            wait(dve, w, "rnc_ready", 2 * g + 2)
                            wait(dve, w, "t1c_ready", g + 1)
                            tt(yc[:, u, 4 * g:4 * g + 4, :], four(t1c, g), four(rnc, g), ALU.mult).then_inc(sem("y_c"), 1)




def merge(nc, dm, io, keep, h_dram, y_dram, out):
    rows, K, T = vector_rows(dm), dm.kt, dm.blk
    D = dm.d // P
    NX = K + dm.wa + dm.hh + dm.vh
    KINDS = 5
    UD, U = KINDS * D, KINDS * D + D
    CH = 2
    FIRST = 4
    WB, XW = BLK // P, BLK // P - 1
    assert dm.wa + dm.hh == K and dm.vh == K and D == K
    hd, yd = h_dram.rearrange("k p n -> p k n"), y_dram.rearrange("k p n -> p k n")
    with ExitStack() as c:
        sb = lambda n, s, d=F32: c.enter_context(nc.sbuf_tensor(n, s, d))
        xs = sb("xs", [P, 2, CH, BLK])
        xh, xl = sb("xh", [P, NX, BLK], F32R), sb("xl", [P, NX, BLK], F32R)
        stage = sb("wo_stage", [P, 2, K, P])
        wh, wl = sb("wo_high", [P, 2, K, P], F32R), sb("wo_low", [P, 2, K, P], F32R)
        sg = sb("sg", [P, 3, BLK])
        tmp = sb("tmp", [P, 2, BLK])
        mh, ml = sb("mh", [P, D, BLK], F32R), sb("ml", [P, D, BLK], F32R)
        ot = sb("ot", [P, D, BLK])
        xw = sb("xw", [P, XW, dm.d])
        fw = sb("fw", [P, dm.d])
        st = sb("st", [P, WB, 3])
        B = [c.enter_context(nc.psum_tensor(f"b_o{i}", [P, BLK], F32)) for i in range(8)]
        sem = lambda n: c.enter_context(nc.semaphore("m_" + n))
        w_in = [sem(f"w_in{s}") for s in range(2)]
        w_high, w_ready, unit_done = Ahead(sem("w_high"), 1), Ahead(sem("w_ready"), 1, 2), Ahead(sem("unit_done"), 1, 2)
        x_in = [sem(f"x_in{s}") for s in range(2)]
        x_high, x_ready = Ahead(sem("x_high"), NX // CH), Ahead(sem("x_ready"), NX // CH)
        gate, prod, summed = Ahead(sem("gate"), 3), Ahead(sem("prod"), 3), Ahead(sem("summed"), 2)
        m_high, merged = Ahead(sem("m_high"), 1), Ahead(sem("merged"), D)
        o_ready, turned, added = Ahead(sem("o_ready"), D), Ahead(sem("turned"), WB), Ahead(sem("added"), 2 * WB)
        stat, out_ready = Ahead(sem("stat"), 3 * WB), Ahead(sem("out_ready"), WB)
        xw_in, xw_out = [sem(f"xw_in{t}") for t in range(WB)], [sem(f"xw_out{t}") for t in range(WB)]
        fw_in, passed, passed_pe = sem("fw_in"), sem("passed"), sem("passed_pe")
        loads = [sum(2 if j % KINDS == 3 else 1 for j in range(m % 2, m + 1, 2)) for m in range(2 * KINDS)]
        per_pair = loads[-1]
        assert loads[-2] == per_pair
        per_block = per_pair * (D // 2) + D // 2

        def unit_no(tb, dp, m):
            return tb * U + (dp * (2 * KINDS) + m)

        with nc.Block() as block:
            @block.sync
            def _(sp):
                fnw = io["final_norm_w"]
                sp.dma_start(fw[:], bass.AP(fnw.tensor, 0, [[0, P], [1, dm.d]])).then_inc(fw_in, 16)
                for t in range(WB):
                    sp.sem_inc(xw_out[t], 16)

                def load_w(tb, dp, m):
                    wait_apart(sp, w_ready.sem, w_ready.at(unit_no(tb, dp, m), -1), passed)
                    kind, cut = m % KINDS, bass.ds(dp * (2 * P) + (m // KINDS) * P, P)
                    slot = stage[:, m % 2, :, :]
                    view = lambda t: t.rearrange("(k p) c -> p k c", p=P)
                    if kind < 3:
                        sp.dma_start(slot, view(io["w_in"][0, :, bass.ds(dp * (2 * P) + (dm.gates + kind * dm.d + (m // KINDS) * P), P)])).then_inc(w_in[m % 2], 16)
                    elif kind == 3:
                        sp.dma_start(slot[:, 0:dm.wa, :], view(io["w_out_a"][0, :, cut])).then_inc(w_in[m % 2], 16)
                        sp.dma_start(slot[:, dm.wa:K, :], view(io["w_out_b"][0, :, cut])).then_inc(w_in[m % 2], 16)
                    else:
                        sp.dma_start(slot, view(io["w_out_c"][0, :, cut])).then_inc(w_in[m % 2], 16)

                def load_x(tb, k):
                    wait_apart(sp, x_ready.sem, x_ready.at(tb, k - 1), passed)
                    cut = bass.ds(tb * BLK, BLK)
                    src = hd[:, CH * k:CH * k + CH, cut] if CH * k < K else yd[:, CH * k - K:CH * k - K + CH, cut]
                    sp.dma_start(xs[:, k % 2, :, :], src).then_inc(x_in[k % 2], 16)

                def load_xw(tb, t):
                    if t < XW:
                        wait_apart(sp, xw_out[t or XW], tb * 16 + 16, passed)
                    else:
                        wait_apart(sp, xw_out[0], tb * 16 + 32, passed)
                    sp.dma_start(xw[:, t % XW, :], io["x"][0, bass.ds(tb * BLK + t * P, P), :]).then_inc(xw_in[t], 16)

                def load_block(tb, more):
                    for m in range(FIRST, 2 * KINDS):
                        load_w(tb, 0, m)
                    with sp.Fori(1, D // 2) as dp:
                        for m in range(2 * KINDS):
                            load_w(tb, dp, m)
                    for t in range(XW):
                        load_xw(tb, t)
                    for e in range(D):
                        wait_apart(sp, w_ready.sem, w_ready.at(tb * U + (UD + e), -1), passed)
                        sp.dma_start(stage[:, e % 2, :, :], io["w_o"][0, :, e * P:(e + 1) * P].rearrange("(k p) c -> p k c", p=P)
                                     ).then_inc(w_in[e % 2], 16)
                        if more and e > 0:
                            for k in range(2 * (e - 1), min(2 * e, NX // CH)):
                                load_x(tb + 1, k)
                    if more:
                        for m in range(FIRST):
                            load_w(tb + 1, 0, m)
                    for t in range(WB):
                        wait_apart(sp, out_ready.sem, out_ready.at(tb, t + 1), passed)
                        sp.dma_start(out[0, bass.ds(tb * BLK + t * P, P), :], xw[:, t % XW, :]).then_inc(xw_out[t], 16)
                        if t == 0:
                            load_xw(tb, XW)

                for k in range(NX // CH):
                    load_x(0, k)
                    if k % 3 == 1:
                        load_w(0, 0, k // 3)
                with sp.Fori(0, T - 1) as tb:
                    load_block(tb, True)
                load_block(T - 1, False)
                for t in range(WB):
                    sp.wait_ge(xw_out[t], 16 * T + 16)

            @block.gpsimd
            def _(pool):
                w_ready.credit(pool)
                with pool.Fori(0, T * U // 2) as i:
                    for s in range(2):
                        n = i * 2 + s
                        pool.wait_ge(w_high.sem, w_high.at(n, 1))
                        nc.gpsimd.tensor_tensor(wl[:, s, :, :], stage[:, s, :, :], wh[:, s, :, :].bitcast(F32), ALU.subtract).then_inc(w_ready.sem, 1)

            @block.tensor
            def _(pe):
                unit_done.credit(pe)
                turned.credit(pe)

                def product(bank, slot, ks, moving, first):
                    high, low = moving
                    for i, k in enumerate(ks):
                        for a, (w, x) in enumerate(((wh, high), (wl, high), (wh, low))):
                            x_ = nc.tensor.matmul(bank[:], w[:, slot, k, :], x[:, first + i, :], start=(i == 0 and a == 0),
                                                  stop=(i == len(ks) - 1 and a == 2))
                    return x_

                with pe.Fori(0, T) as tb:
                    with pe.Fori(0, D // 2) as dp:
                        for m in range(2 * KINDS):
                            kind, slot, tile = m % KINDS, m % 2, tb * D + (dp * 2 + m // KINDS)
                            pe.wait_ge(w_ready.sem, w_ready.at(unit_no(tb, dp, m), 1))
                            pe.wait_ge(x_ready.sem, x_ready.at(tb, (K, 2 * K, 3 * K)[max(kind - 2, 0)] // CH))
                            if kind < 3:
                                pe.wait_ge(gate.sem, gate.at(tile, kind - 2))
                                last = product(B[kind], slot, range(K), (xh, xl), 0)
                            elif kind == 3:
                                pe.wait_ge(added.sem, added.at(tb, 0))
                                pe.wait_ge(prod.sem, prod.at(tile, -1))
                                product(B[3], slot, range(dm.wa), (xh, xl), K)
                                last = product(B[4], slot, range(dm.wa, K), (xh, xl), K + dm.wa)
                            else:
                                pe.wait_ge(prod.sem, prod.at(tile, 0))
                                last = product(B[5], slot, range(K), (xh, xl), 2 * K)
                            last.then_inc(unit_done.sem, 1)
                    wait_apart(pe, merged.sem, merged.at(tb, D), passed_pe)
                    with pe.Fori(0, D // 2) as ep:
                        for s in range(2):
                            pe.wait_ge(w_ready.sem, w_ready.at(tb * U + (ep * 2 + (UD + s)), 1))
                            pe.wait_ge(o_ready.sem, ep * 2 + (tb * D + (D + s - 1)))
                            product(B[6 + s], s, range(K), (mh, ml), 0).then_inc(unit_done.sem, 1)
                    pe.wait_ge(o_ready.sem, o_ready.at(tb, D))
                    pe.wait_ge(prod.sem, prod.at(tb * D + D, 0))
                    for t in range(WB):
                        if t >= 2:
                            pe.wait_ge(added.sem, added.at(tb, 2 * (t - 1)))
                        for e in range(D):
                            x_ = nc.tensor.transpose(B[4 + 2 * (t % 2) + e // 4][:, (e % 4) * P:(e % 4 + 1) * P], ot[:, e, t * P:(t + 1) * P], keep["ident"][:])
                        x_.then_inc(turned.sem, 1)

            @block.scalar
            def _(act):
                for s in (w_high, gate, o_ready, stat):
                    s.credit(act)

                def split(n, slot, value):
                    act.wait_ge(w_in[slot], value)
                    act.wait_ge(unit_done.sem, unit_done.at(n, -1))
                    nc.scalar.activation(wh[:, slot, :, :], stage[:, slot, :, :], ACT.Copy).then_inc(w_high.sem, 1)

                def block_steps(tb, more):
                    nc.scalar.preload_act_table_set(SIGMOID_TABLES)
                    block_loads = tb * (16 * per_block)
                    with act.Fori(0, D // 2) as dp:
                        for m in range(2 * KINDS):
                            n, tile = unit_no(tb, dp, m), tb * D + (dp * 2 + m // KINDS)
                            upto = loads[m + 2] if m + 2 < 2 * KINDS else per_pair + 1
                            split(n + 2, m % 2, block_loads + (dp * (16 * per_pair) + 16 * upto))
                            if m % KINDS < 3:
                                act.wait_ge(unit_done.sem, unit_done.at(n, 1))
                                act.wait_ge(prod.sem, prod.at(tile, 0))
                                at = dp * 2 + (rows["b_gate"] + (m % KINDS) * D + m // KINDS)
                                nc.scalar.activation(sg[:, m % KINDS, :], B[m % KINDS][:], ACT.Sigmoid,
                                                     bias=keep["cols"][:, bass.ds(at, 1)]).then_inc(gate.sem, 1)
                    all_pairs = 16 * per_pair * (D // 2)

                    def out_tile(ep, s, next_unit):
                        n = tb * U + (ep * 2 + (UD + s))
                        if next_unit:
                            split(n + 2, s, block_loads + (ep * 16 + (all_pairs + 32)))
                        act.wait_ge(unit_done.sem, unit_done.at(n, 1))
                        act.wait_ge(turned.sem, turned.at(tb, 0))
                        nc.scalar.activation(ot[:, bass.ds(ep * 2 + s, 1), :], B[6 + s][:], ACT.Copy).then_inc(o_ready.sem, 1)

                    with act.Fori(0, D // 2 - 1) as ep:
                        for s in range(2):
                            out_tile(ep, s, True)
                    for s in range(2):
                        out_tile(D // 2 - 1, s, more)
                    nc.scalar.preload_act_table_set(TABLES)
                    for t in range(WB):
                        act.wait_ge(added.sem, added.at(tb, 2 * t + 2))
                        nc.scalar.activation(tmp[:].rearrange("p a n -> p (a n)"), xw[:, t % XW, :], ACT.Square, accum_out=st[:, t, 0:1]).then_inc(stat.sem, 1)
                        act.wait_ge(stat.sem, stat.at(tb, 3 * t + 1))
                        nc.scalar.activation(st[:, t, 1:2], st[:, t, 0:1], ACT.Ln, scale=1.0 / dm.d, bias=keep["eps"][:, 0:1]).then_inc(stat.sem, 1)
                        act.wait_ge(stat.sem, stat.at(tb, 3 * t + 2))
                        nc.scalar.activation(st[:, t, 2:3], st[:, t, 1:2], ACT.Exp, scale=NEG_HALF).then_inc(stat.sem, 1)

                for s in range(2):
                    split(s, s, 16)
                with act.Fori(0, T - 1) as tb:
                    block_steps(tb, True)
                block_steps(T - 1, False)

            @block.vector
            def _(dve):
                for s in (x_high, x_ready, prod, summed, m_high, merged, added, out_ready):
                    s.credit(dve)
                tt, ts = nc.vector.tensor_tensor, nc.vector.tensor_scalar
                dve.wait_ge(fw_in, 16)

                def split_x(tb):
                    for k in range(NX // CH):
                        dve.wait_ge(x_in[k % 2], tb * (16 * (NX // CH // 2)) + (16 * (k // 2) + 16))
                        cut = slice(CH * k, CH * k + CH)
                        ts(xh[:, cut, :], xs[:, k % 2, :, :], 1.0, None, ALU.mult).then_inc(x_high.sem, 1)
                        dve.wait_ge(x_high.sem, x_high.at(tb, k + 1))
                        tt(xl[:, cut, :], xs[:, k % 2, :, :], xh[:, cut, :].bitcast(F32), ALU.subtract).then_inc(x_ready.sem, 1)

                def block_steps(tb, more):
                    with dve.Fori(0, D // 2) as dp:
                        for dd in range(2):
                            tile = tb * D + (dp * 2 + dd)
                            ab = unit_no(tb, dp, KINDS * dd + 3)
                            dve.wait_ge(gate.sem, gate.at(tile, 3))
                            dve.wait_ge(unit_done.sem, unit_done.at(ab, 1))
                            dve.wait_ge(merged.sem, merged.at(tb, 0) + (dp * 2 + dd))
                            tt(tmp[:, 0, :], B[3][:], sg[:, 0, :], ALU.mult).then_inc(prod.sem, 1)
                            tt(tmp[:, 1, :], B[4][:], sg[:, 1, :], ALU.mult).then_inc(prod.sem, 1)
                            dve.wait_ge(prod.sem, prod.at(tile, 2))
                            tt(tmp[:, 0, :], tmp[:, 0, :], tmp[:, 1, :], ALU.add).then_inc(summed.sem, 1)
                            dve.wait_ge(unit_done.sem, unit_done.at(ab, 2))
                            dve.wait_ge(summed.sem, summed.at(tile, 1))
                            tt(tmp[:, 1, :], B[5][:], sg[:, 2, :], ALU.mult).then_inc(prod.sem, 1)
                            dve.wait_ge(prod.sem, prod.at(tile, 3))
                            tt(tmp[:, 0, :], tmp[:, 0, :], tmp[:, 1, :], ALU.add).then_inc(summed.sem, 1)
                            dve.wait_ge(summed.sem, summed.at(tile, 2))
                            at = bass.ds(dp * 2 + dd, 1)
                            ts(mh[:, at, :], tmp[:, 0:1, :], 1.0, None, ALU.mult).then_inc(m_high.sem, 1)
                            dve.wait_ge(m_high.sem, m_high.at(tile, 1))
                            tt(ml[:, at, :], tmp[:, 0:1, :], mh[:, at, :].bitcast(F32), ALU.subtract).then_inc(merged.sem, 1)
                    if more:
                        dve.wait_ge(unit_done.sem, unit_done.at(tb * U + UD, 0))
                        split_x(tb + 1)
                    for t in range(WB + 1):
                        if t < WB:
                            dve.wait_ge(turned.sem, turned.at(tb, t + 1))
                            dve.wait_ge(xw_in[t], tb * 16 + 16)
                            for b in range(2):
                                half = xw[:, t % XW, b * BLK:(b + 1) * BLK]
                                tt(half, B[4 + 2 * (t % 2) + b][:], half, ALU.add).then_inc(added.sem, 1)
                        if t > 0:
                            x_row = xw[:, (t - 1) % XW, :]
                            dve.wait_ge(stat.sem, stat.at(tb, 3 * t))
                            nc.vector.scalar_tensor_tensor(x_row, x_row, st[:, t - 1, 2:3], fw[:], ALU.mult, ALU.mult).then_inc(out_ready.sem, 1)

                split_x(0)
                with dve.Fori(0, T - 1) as tb:
                    block_steps(tb, True)
                block_steps(T - 1, False)




def hybrid_trunk(nc, io, out):
    dm = Dims(io["x"], io["w_in"], io["w_out_a"], io["w_out_b"], io["w_out_c"])
    h_dram = nc.dram_tensor("h_scratch", [dm.kt, P, dm.seq], F32).ap()
    s_dram = nc.dram_tensor("branch_scratch", [branch_tiles(dm)["end"], P, dm.seq], F32).ap()
    y_dram = nc.dram_tensor("y_scratch", [dm.wa + dm.hh + dm.vh, P, dm.seq], F32).ap()
    with ExitStack() as c:
        sb = lambda n, s, d=F32: c.enter_context(nc.sbuf_tensor(n, s, d))
        keep = {"ident": sb("ident", [P, P]), "ones": sb("ones", [P, P]), "cols": sb("cols", [P, P]),
                "eps": sb("eps", [P, 1]), "a_log": sb("a_log_t", [P, dm.vh]), "dt_bias": sb("dt_bias_t", [P, dm.vh]),
                "lb": sb("lb", [P, dm.hh]), "one_less_lb": sb("one_less_lb", [P, dm.hh]), "head_w": sb("head_w", [P, 2]),
                "ab": sb("ab", [P, (dm.win + 1) * 2 * dm.vh]),
                "masks": {"causal": sb("causal", [P, P]), "later": sb("later", [P, P])}}
        constants(nc, dm, io, keep)
        with nc.sbuf_tensor("hh", [P, dm.kt, dm.seq], F32R) as hh, nc.sbuf_tensor("hl", [P, dm.kt, dm.seq], F32R) as hl:
            norm_and_transpose(nc, dm, io, keep, hh, hl, h_dram)
            project(nc, dm, io, keep, hh, hl, s_dram, y_dram)
        recur(nc, dm, keep, s_dram, y_dram)
        merge(nc, dm, io, keep, h_dram, y_dram, out)


_INS = ["x", "norm_w", "w_in", "b_gate", "conv_a", "conv_c", "a_log", "dt_bias", "lower_bounds",
        "hgrn_norm_w", "gdn_norm_w", "w_out_a", "w_out_b", "w_out_c", "w_o", "final_norm_w"]


def kernel(**inputs):
    import numpy as _np
    import concourse.bacc as _bacc
    from concourse import mybir as _mybir
    from concourse.bass_utils import run_bass_kernel_spmd as _run

    nc = _bacc.Bacc("TRN2", target_bir_lowering=False, num_devices=1)
    arrays, io = {}, {}
    for name in _INS:
        a = _np.ascontiguousarray(inputs[name])
        arrays[f"in_{name}_dram"] = a
        io[name] = nc.dram_tensor(f"in_{name}_dram", a.shape, _mybir.dt.from_np(a.dtype), kind="ExternalInput").ap()
    out = nc.dram_tensor("out_0_dram", inputs["x"].shape, _mybir.dt.float32, kind="ExternalOutput").ap()
    hybrid_trunk(nc, io, out)
    r = _run(nc, [arrays], core_ids=[0])
    return r.results[0]["out_0_dram"]
```
